# Optimizing a Trainium2 kernel written in Bass

```python
import jax, jax.numpy as jnp
from jax import lax
import numpy as np

D_MODEL = 1024
BATCH = 1
SEQ = 512
DEPTH = 1

MLA_HEADS = 8
MLA_NOPE_DIM = 64
MLA_ROPE_DIM = 32
MLA_V_DIM = 64
MLA_Q_RANK = 256
MLA_KV_RANK = 128
MOBA_HEADS = 8
MOBA_HEAD_DIM = 64
MOBA_BLOCK = 256
MOBA_TOPK = 3
MOBA_Q_CHUNK = 32
D_FF = 4 * D_MODEL
ROPE_THETA = 10000.0
NORM_EPS = 1e-6
Q_BLOCK = 128
NEG_INF = -1e30

MLA_WIDTH = MLA_HEADS * MLA_V_DIM
MOBA_WIDTH = MOBA_HEADS * MOBA_HEAD_DIM
MIX_WIDTH = MLA_WIDTH + MOBA_WIDTH
IN_COLS = MLA_Q_RANK + MLA_KV_RANK + MLA_ROPE_DIM + 3 * MOBA_WIDTH

kernel_name = 'hymba_mla_moba_sandwich_layer'

def rms_norm(x, g):
    xf = x.astype(jnp.float32)
    y = xf * lax.rsqrt(jnp.mean(xf * xf, axis=-1, keepdims=True) + NORM_EPS)
    return (y * g.astype(jnp.float32)).astype(x.dtype)

def rope(x, pos):
    half = x.shape[-1] // 2
    inv_freq = 1.0 / (ROPE_THETA ** (jnp.arange(half, dtype=jnp.float32) / half))
    ang = pos.astype(jnp.float32)[:, None] * inv_freq[None, :]
    cos = jnp.cos(ang).astype(x.dtype)
    sin = jnp.sin(ang).astype(x.dtype)
    x1 = x[..., :half]
    x2 = x[..., half:]
    return jnp.concatenate([x1 * cos - x2 * sin, x2 * cos + x1 * sin], axis=-1)

def causal_dense_attention(q, k, v, scale):
    B, H, S, Dq = q.shape
    Dv = v.shape[-1]
    nq = S // Q_BLOCK
    qb = q.reshape(B, H, nq, Q_BLOCK, Dq).transpose(2, 0, 1, 3, 4)
    k_pos = jnp.arange(S)

    def one(args):
        q_blk, start = args
        s = jnp.einsum('bhqd,bhkd->bhqk', q_blk, k).astype(jnp.float32) * scale
        q_pos = start + jnp.arange(Q_BLOCK)
        s = jnp.where(k_pos[None, :] <= q_pos[:, None], s, NEG_INF)
        p = jax.nn.softmax(s, axis=-1).astype(v.dtype)
        return jnp.einsum('bhqk,bhkd->bhqd', p, v)

    out = lax.map(one, (qb, jnp.arange(nq, dtype=jnp.int32) * Q_BLOCK))
    return out.transpose(1, 2, 0, 3, 4).reshape(B, H, S, Dv)

def mla_attention(c_q, c_kv, k_r, q_norm_g, w_q_up, kv_norm_g, w_kv_up, pos):
    B, S, _ = c_q.shape
    q = (rms_norm(c_q, q_norm_g) @ w_q_up).reshape(B, S, MLA_HEADS, MLA_NOPE_DIM + MLA_ROPE_DIM)
    q = q.transpose(0, 2, 1, 3)
    q_nope = q[..., :MLA_NOPE_DIM]
    q_rope = rope(q[..., MLA_NOPE_DIM:], pos)
    kv = (rms_norm(c_kv, kv_norm_g) @ w_kv_up).reshape(B, S, MLA_HEADS, MLA_NOPE_DIM + MLA_V_DIM)
    kv = kv.transpose(0, 2, 1, 3)
    k_nope = kv[..., :MLA_NOPE_DIM]
    v = kv[..., MLA_NOPE_DIM:]
    k_rope = rope(k_r[:, None, :, :], pos)
    k_rope = jnp.broadcast_to(k_rope, (B, MLA_HEADS, S, MLA_ROPE_DIM))
    q_full = jnp.concatenate([q_nope, q_rope], axis=-1)
    k_full = jnp.concatenate([k_nope, k_rope], axis=-1)
    scale = (MLA_NOPE_DIM + MLA_ROPE_DIM) ** -0.5
    return causal_dense_attention(q_full, k_full, v, scale)

def moba_attention(q, k, v):
    B, H, S, D = q.shape
    nb = -(-S // MOBA_BLOCK)
    s_pad = nb * MOBA_BLOCK
    pad = ((0, 0), (0, 0), (0, s_pad - S), (0, 0))
    k_p = jnp.pad(k, pad)
    v_p = jnp.pad(v, pad)
    k_blocks = k_p.reshape(B, H, nb, MOBA_BLOCK, D)
    v_blocks = v_p.reshape(B, H, nb, MOBA_BLOCK, D)
    k_mean = jnp.mean(k_blocks.astype(jnp.float32), axis=3)
    top = min(MOBA_TOPK, nb)
    n_chunks = S // MOBA_Q_CHUNK
    qc = q.reshape(B, H, n_chunks, MOBA_Q_CHUNK, D).transpose(2, 0, 1, 3, 4)
    b_idx = jnp.arange(B)[:, None, None, None]
    h_idx = jnp.arange(H)[None, :, None, None]
    blk_ids = jnp.arange(nb)
    offs = jnp.arange(MOBA_BLOCK)
    scale = D ** -0.5

    def one(args):
        q_blk, start = args
        cur = start // MOBA_BLOCK
        gate = jnp.einsum('bhqd,bhnd->bhqn', q_blk.astype(jnp.float32), k_mean)
        gate = jnp.where(blk_ids < cur, gate, NEG_INF)
        _, sel = lax.top_k(gate, top)
        sel_valid = sel < cur
        k_sel = k_blocks[b_idx, h_idx, sel]
        v_sel = v_blocks[b_idx, h_idx, sel]
        s_sel = jnp.einsum('bhqd,bhqnkd->bhqnk', q_blk, k_sel).astype(jnp.float32) * scale
        s_sel = jnp.where(sel_valid[..., None], s_sel, NEG_INF)
        s_sel = s_sel.reshape(B, H, MOBA_Q_CHUNK, top * MOBA_BLOCK)
        k_own = lax.dynamic_slice_in_dim(k_p, cur * MOBA_BLOCK, MOBA_BLOCK, axis=2)
        v_own = lax.dynamic_slice_in_dim(v_p, cur * MOBA_BLOCK, MOBA_BLOCK, axis=2)
        s_own = jnp.einsum('bhqd,bhkd->bhqk', q_blk, k_own).astype(jnp.float32) * scale
        q_pos = start + jnp.arange(MOBA_Q_CHUNK)
        k_pos = cur * MOBA_BLOCK + offs
        s_own = jnp.where(k_pos[None, :] <= q_pos[:, None], s_own, NEG_INF)
        p = jax.nn.softmax(jnp.concatenate([s_sel, s_own], axis=-1), axis=-1).astype(v.dtype)
        p_sel = p[..., :top * MOBA_BLOCK].reshape(B, H, MOBA_Q_CHUNK, top, MOBA_BLOCK)
        p_own = p[..., top * MOBA_BLOCK:]
        return (jnp.einsum('bhqnk,bhqnkd->bhqd', p_sel, v_sel)
                + jnp.einsum('bhqk,bhkd->bhqd', p_own, v_own))

    out = lax.map(one, (qc, jnp.arange(n_chunks, dtype=jnp.int32) * MOBA_Q_CHUNK))
    return out.transpose(1, 2, 0, 3, 4).reshape(B, H, S, D)

def setup_inputs(seed: int = 0) -> dict:
    key = jax.random.key(seed)
    ks = jax.random.split(key, 14)

    def nrm(k, shape, scale):
        return jax.random.normal(k, shape, jnp.float32) * scale

    def gain(k, n):
        return 1.0 + 0.05 * jax.random.normal(k, (DEPTH, n), jnp.float32)

    return {
        'x': nrm(ks[0], (BATCH, SEQ, D_MODEL), 1.0),
        'attn_pre_g': gain(ks[1], D_MODEL),
        'w_in': nrm(ks[2], (DEPTH, D_MODEL, IN_COLS), D_MODEL ** -0.5),
        'mla_q_norm_g': gain(ks[3], MLA_Q_RANK),
        'w_mla_q_up': nrm(ks[4], (DEPTH, MLA_Q_RANK, MLA_HEADS * (MLA_NOPE_DIM + MLA_ROPE_DIM)), MLA_Q_RANK ** -0.5),
        'mla_kv_norm_g': gain(ks[5], MLA_KV_RANK),
        'w_mla_kv_up': nrm(ks[6], (DEPTH, MLA_KV_RANK, MLA_HEADS * (MLA_NOPE_DIM + MLA_V_DIM)), MLA_KV_RANK ** -0.5),
        'w_out': nrm(ks[7], (DEPTH, MIX_WIDTH, D_MODEL), MIX_WIDTH ** -0.5),
        'attn_post_g': gain(ks[8], D_MODEL),
        'mlp_pre_g': gain(ks[9], D_MODEL),
        'w_up': nrm(ks[10], (DEPTH, D_MODEL, D_FF), D_MODEL ** -0.5),
        'w_down': nrm(ks[11], (DEPTH, D_FF, D_MODEL), D_FF ** -0.5),
        'mlp_post_g': gain(ks[12], D_MODEL),
    }

def reference(x, attn_pre_g, w_in, mla_q_norm_g, w_mla_q_up, mla_kv_norm_g, w_mla_kv_up,
              w_out, attn_post_g, mlp_pre_g, w_up, w_down, mlp_post_g):
    B, S, _ = x.shape
    pos = jnp.arange(S, dtype=jnp.int32)
    s1 = MLA_Q_RANK
    s2 = s1 + MLA_KV_RANK
    s3 = s2 + MLA_ROPE_DIM
    h = x
    for l in range(DEPTH):
        u = rms_norm(h, attn_pre_g[l])
        proj = u @ w_in[l]
        c_q = proj[..., :s1]
        c_kv = proj[..., s1:s2]
        k_r = proj[..., s2:s3]
        moba_qkv = proj[..., s3:].reshape(B, S, 3, MOBA_HEADS, MOBA_HEAD_DIM)
        moba_qkv = moba_qkv.transpose(2, 0, 3, 1, 4)
        mla_o = mla_attention(c_q, c_kv, k_r, mla_q_norm_g[l], w_mla_q_up[l],
                              mla_kv_norm_g[l], w_mla_kv_up[l], pos)
        moba_o = moba_attention(rope(moba_qkv[0], pos), rope(moba_qkv[1], pos), moba_qkv[2])
        mix = jnp.concatenate([
            mla_o.transpose(0, 2, 1, 3).reshape(B, S, MLA_WIDTH),
            moba_o.transpose(0, 2, 1, 3).reshape(B, S, MOBA_WIDTH)], axis=-1)
        h = h + rms_norm(mix @ w_out[l], attn_post_g[l])
        u = rms_norm(h, mlp_pre_g[l])
        a = jnp.square(jax.nn.relu(u @ w_up[l]))
        h = h + rms_norm(a @ w_down[l], mlp_post_g[l])
    return h


_drawn_inputs = setup_inputs


def setup_inputs(seed=0):
    import zlib

    import numpy as np

    out = dict(_drawn_inputs(seed))
    spreads = {}
    factors = {}
    for name, (base, spread) in spreads.items():
        noise = np.random.default_rng([zlib.crc32(name.encode()), seed]).standard_normal(out[name].shape)
        drawn = base * np.exp(spread * noise) if base else spread * noise
        out[name] = __import__('jax').numpy.asarray(drawn.astype(out[name].dtype))
    for name, factor in factors.items():
        out[name] = (out[name] * factor).astype(out[name].dtype)
    return out
```

```python
from contextlib import ExitStack

import concourse.bass as bass
from concourse import mybir

F32 = mybir.dt.float32
F32R = mybir.dt.float32r
BF16 = mybir.dt.bfloat16
ALU = mybir.AluOpType
ACT = mybir.ActivationFunctionType
AX_X = mybir.AxisListType.X

P = 128
EPS = 1e-6
NEG = -1e30
NOPE, ROPE, VD = 64, 32, 64
HEADS = 8
MOBA_D = 64
TOP = 512


def build(nc, x, attn_pre_g, w_in, mla_q_norm_g, w_mla_q_up, mla_kv_norm_g, w_mla_kv_up, w_out,
          attn_post_g, mlp_pre_g, w_up, w_down, mlp_post_g, rope_table, out):
    S, D = x.shape[1], x.shape[2]
    F = w_up.shape[2]
    QR, KVR = w_mla_q_up.shape[1], w_mla_kv_up.shape[1]
    NT = S // P
    ND = D // P
    NF = F // P
    CA = QR + KVR + ROPE
    HW = HEADS * MOBA_D
    QH = NOPE + ROPE
    CW = 2048
    NH = 2 * HEADS
    SCALE = [float(QH) ** -0.5] * HEADS + [float(MOBA_D) ** -0.5] * HEADS
    assert (S, D, F, NT, CA) == (512, 1024, 4096, 4, 416)

    x_v = x[0].rearrange("(t p) d -> t p d", p=P)
    out_v = out[0].rearrange("(t p) d -> t p d", p=P)
    w_in_v = w_in[0].rearrange("(k p) n -> p k n", p=P)
    w_q_v = w_mla_q_up[0].rearrange("(k p) n -> p k n", p=P)
    w_out_v = w_out[0].rearrange("(k p) n -> p k n", p=P)
    w_up_v = w_up[0].rearrange("(k p) n -> p k n", p=P)
    w_down_v = w_down[0].rearrange("(k p) n -> p k n", p=P)

    IN_CH = [0, 1, 2, 3, 4, 5, 8, 9]
    Q_CH, KV_CH = 6, 7
    OUT_CH = [10, 11, 12, 13]
    UP_CH = 14
    DOWN_CH = UP_CH + NF // 2
    GROUP_COLS = [(0, CA), (CA, HW), (CA + HW, HW), (CA + 2 * HW, HW)]

    with ExitStack() as ctx:
        def sb(name, shape, dt=F32, stack=ctx):
            return stack.enter_context(nc.sbuf_tensor(name, shape, dt))

        def sem(name):
            return ctx.enter_context(nc.semaphore(name))

        h_sb = sb("h_sb", [P, NT, D])
        uT_hi = sb("uT_hi", [P, ND, S], F32R)
        uT_lo = sb("uT_lo", [P, ND, S], F32R)
        raw = [sb(f"w_raw{i}", [P, CW]) for i in range(2)]
        w_hi = [sb(f"w_hi{i}", [P, CW], F32R) for i in range(2)]
        w_lo = [sb(f"w_lo{i}", [P, CW], F32R) for i in range(2)]
        pre_g = sb("pre_g", [P, D])
        post_g = sb("post_g", [P, D])
        ident = sb("ident", [P, P])
        ident_b = sb("ident_b", [P, P], BF16)
        mask_b = sb("mask_b", [P, P], BF16)
        half = sb("half", [P, 1])
        stat = sb("stat", [P, 6, NT, 4])
        un = sb("un", [P, 2, D])
        att, pre = ExitStack(), ExitStack()
        cT_hi = sb("cT_hi", [P, 3, S], F32R, stack=att)
        cT_lo = sb("cT_lo", [P, 3, S], F32R, stack=att)
        wkv_hi = sb("wkv_hi", [P, HEADS * P], F32R, stack=att)
        wkv_lo = sb("wkv_lo", [P, HEADS * P], F32R, stack=att)
        q_nat = sb("q_nat", [P, NT, HEADS * QH], stack=att)
        mq_nat = sb("mq_nat", [P, NT, HW], stack=att)
        mk_nat = sb("mk_nat", [P, NT, HW], stack=att)
        v_sb = sb("v_sb", [P, 2, NT, HW], stack=att)
        qT = [sb(f"qT{i}", [P, S], stack=att) for i in range(2)]
        kT = [sb(f"kT{i}", [P, S], stack=att) for i in range(2)]
        mx = sb("mx", [P, 2, NT], stack=att)
        nb = sb("nb", [P, 2, NT], stack=att)
        rs = sb("rs", [P, 2, NT], stack=att)
        ri = sb("ri", [P, 2, NT], stack=att)
        lat_g = sb("lat_g", [P, QR + KVR], stack=pre)
        rope_sb = sb("rope_sb", [P, NT, rope_table.shape[1]], stack=pre)
        cn = sb("cn", [P, NT, QR + KVR], stack=pre)
        kr = sb("kr", [P, NT, ROPE], stack=pre)
        krr = sb("krr", [P, NT, ROPE], stack=pre)
        rt1 = sb("rt1", [P, 2, HW], stack=pre)
        rt2 = sb("rt2", [P, 2, HW], stack=pre)
        pre.close()
        probs = [sb(f"probs{i}", [P, NT * (NT + 1) // 2 * P], stack=att) for i in range(2)]
        pT = [sb(f"pT{i}", [P, NT * (NT + 1) // 2 * P], stack=att) for i in range(2)]
        att.close()
        act_sb = sb("act_sb", [P, NF, S])
        relu = sb("relu", [P, 2, S])
        a_hi = [sb(f"a_hi{i}", [P, 2, S], F32R) for i in range(2)]
        a_lo = [sb(f"a_lo{i}", [P, 2, S], F32R) for i in range(2)]

        ps = [ctx.enter_context(nc.psum_tensor(f"bank{b}", [P, TOP], F32)) for b in range(8)]

        x_in = [sem(f"x{t}_in") for t in range(NT)]
        g_pre_in, g_post_in, tab_in, lat_in = sem("g_pre_in"), sem("g_post_in"), sem("tab_in"), sem("lat_in")
        raw_in = [sem(f"raw{i}_in") for i in range(2)]
        wh_ready = sem("wh_ready")
        w_ready = sem("w_ready")
        w_used = sem("w_used")
        cst = sem("cst")
        cst2 = sem("cst2")
        sq = sem("sq")
        pool_step = sem("pool_step")
        dve_step = sem("dve_step")
        rstd = sem("rstd")
        un_ready = sem("un_ready")
        uT_full = sem("uT_full")
        uh = sem("uh")
        ul = sem("ul")
        proj = sem("proj")
        kr_c, krr_ready = sem("kr_c"), sem("krr_ready")
        cn_ready = sem("cn_ready")
        rope_m = sem("rope_m")
        roped = sem("roped")
        cT_full, krT_full = sem("cT_full"), sem("krT_full")
        ch, cl = sem("ch"), sem("cl")
        krT_c = sem("krT_c")
        qup, qup_c, qk_rope = sem("qup"), sem("qup_c"), sem("qk_rope")
        q_roped = sem("q_roped")
        vup = sem("vup")
        v_ready = sem("v_ready")
        qT_full, kT_full, qT_c, kT_c = sem("qT_full"), sem("kT_full"), sem("qT_c"), sem("kT_c")
        s_full, s_max, s_nb, s_exp = sem("s_full"), sem("s_max"), sem("s_nb"), sem("s_exp")
        s_ri, s_norm = sem("s_ri"), sem("s_norm")
        pT_full, pT_act, pT_dve = sem("pT_full"), sem("pT_act"), sem("pT_dve")
        o_full, o_hi, o_lo = sem("o_full"), sem("o_hi"), sem("o_lo")
        y_full = sem("y_full")
        y_s = sem("y_s")
        h_ready = sem("h_ready")
        up_full, relu_c, a_ready = sem("up_full"), sem("relu_c"), sem("a_ready")
        ah, al, a_used = sem("ah"), sem("al"), sem("a_used")
        out_done = sem("out_done")

        def p_off(t):
            return P * (t * (t + 1) // 2)

        PT_OFF = [0, TOP, 2 * TOP, 2 * TOP - P]

        def slot(i):
            return i % 2 if i < HEADS else (i // 2) % 2

        def before(i):
            return i - 2 if i <= HEADS else i - 3

        def prepared(i):
            return i < NH and (i < HEADS or i % 2 == 0)

        def preps(i):
            return i + 1 if i < HEADS else HEADS + (i - HEADS) // 2 + 1

        S_AT = [(0, 0), (1, 0), (0, P), (2, 0)]
        S_ORDER = [3, 1, 0, 2]
        PT_AT = [(3, 0), (4, 0), (5, 0), (4, 3 * P)]
        PT_ORDER = [0, 1, 3, 2]

        block = ctx.enter_context(nc.Block())

        @block.sync
        def _(sp):
            def chunk(r, src, n, wait=True):
                if r >= 2 and wait:
                    sp.wait_ge(w_ready, r - 1)
                k = src.shape[1]
                dst = raw[r % 2][:, 0:n].rearrange("p (k n) -> p k n", k=k)
                sp.dma_start(dst, src).then_inc(raw_in[r % 2], 16)

            def in_chunk(i):
                g, part = i // 2, i % 2
                c0, n = GROUP_COLS[g]
                chunk(IN_CH[i], w_in_v[:, 4 * part:4 * part + 4, c0:c0 + n], 4 * n)

            sp.dma_start(h_sb[:, 0, :], x_v[0]).then_inc(x_in[0], 16)
            sp.dma_start(pre_g[:, :], attn_pre_g.to_broadcast([P, D])).then_inc(g_pre_in, 16)
            in_chunk(0)
            for t in range(1, NT):
                sp.dma_start(h_sb[:, t, :], x_v[t]).then_inc(x_in[t], 16)
            in_chunk(1)
            sp.dma_start(rope_sb[:, :, :], rope_table.rearrange("(t p) c -> p t c", p=P)).then_inc(tab_in, 16)
            sp.dma_start(lat_g[:, 0:QR], mla_q_norm_g.to_broadcast([P, QR])).then_inc(lat_in, 16)
            sp.dma_start(lat_g[:, QR:], mla_kv_norm_g.to_broadcast([P, KVR])).then_inc(lat_in, 16)
            for i in range(2, 6):
                in_chunk(i)
            chunk(Q_CH, w_q_v, 2 * HEADS * QH)
            chunk(KV_CH, w_mla_kv_up.rearrange("o p n -> p o n"), HEADS * P)
            in_chunk(6)
            in_chunk(7)
            sp.dma_start(post_g[:, :], attn_post_g.to_broadcast([P, D])).then_inc(g_post_in, 16)
            sp.wait_ge(un_ready, NT)
            sp.dma_start(pre_g[:, :], mlp_pre_g.to_broadcast([P, D])).then_inc(g_pre_in, 16)
            for i, r in enumerate(OUT_CH):
                chunk(r, w_out_v[:, 2 * i:2 * i + 2, :], CW)
            with sp.Fori(0, NF // 4) as i:
                for j in range(2):
                    sp.wait_ge(w_ready, i * 2 + (UP_CH + j - 1))
                    sp.dma_start(raw[j][:, :].rearrange("p (k n) -> p k n", k=ND),
                                 w_up_v[:, :, bass.ds(i * 512 + j * 256, 256)]).then_inc(raw_in[j], 16)
            with sp.Fori(0, NF // 4) as i:
                for j in range(2):
                    sp.wait_ge(w_ready, i * 2 + (DOWN_CH + j - 1))
                    sp.dma_start(raw[j][:, :].rearrange("p (k n) -> p k n", k=2),
                                 w_down_v[:, bass.ds(i * 4 + 2 * j, 2), :]).then_inc(raw_in[j], 16)
            sp.wait_ge(y_s, 2 * NT)
            sp.dma_start(post_g[:, :], mlp_post_g.to_broadcast([P, D])).then_inc(g_post_in, 16)
            for t in range(NT):
                sp.wait_ge(h_ready, NT + t + 1)
                sp.dma_start(out_v[t], h_sb[:, t, :]).then_inc(out_done, 16)
            sp.wait_ge(out_done, 16 * NT)

        @block.gpsimd
        def _(pool):
            nc.gpsimd.memset(ident[:, :], 0.0).then_inc(cst2, 1)
            nc.gpsimd.memset(ident_b[:, :], 0.0).then_inc(cst2, 1)
            nc.gpsimd.memset(mask_b[:, :], 0.0).then_inc(cst2, 1)
            nc.gpsimd.memset(half[:, :], -0.5).then_inc(cst2, 1)
            pool.wait_ge(cst2, 4)
            for m in (ident, ident_b):
                nc.gpsimd.affine_select(out=m[:, :], in_=m[:, :], compare_op=ALU.not_equal, fill=1.0, base=0,
                                        pattern=[[-1, P]], channel_multiplier=1).then_inc(cst, 1)
            nc.gpsimd.affine_select(out=mask_b[:, :], in_=mask_b[:, :], compare_op=ALU.is_ge, fill=NEG, base=0,
                                    pattern=[[-1, P]], channel_multiplier=1).then_inc(cst, 1)
            own = [0]

            def step(ins):
                own[0] += 1
                ins.then_inc(pool_step, 1)
                pool.wait_ge(pool_step, own[0])

            def rms(norm, t, n, parts, wait, last=True):
                if wait:
                    pool.wait_ge(sq, wait)
                s = stat[:, norm, t, :]
                src = s[:, 0:1]
                if parts == 2:
                    step(nc.gpsimd.tensor_tensor(s[:, 2:3], s[:, 0:1], s[:, 1:2], ALU.add))
                    src = s[:, 2:3]
                step(nc.gpsimd.tensor_scalar(s[:, 2:3], src, 1.0 / n, EPS, ALU.mult, ALU.add))
                nc.gpsimd.tensor_tensor(s[:, 3:4], s[:, 2:3], half[:, :], ALU.pow).then_inc(rstd, 1)

            for t in range(NT):
                rms(0, t, D, 1, t + 1)
            for t in range(NT):
                rms(1, t, QR, 1, NT + 2 * t + 1)
                rms(2, t, KVR, 1, NT + 2 * t + 2)
            for n in range(2 * NT):
                t = n % NT
                pool.wait_ge(rope_m, n + 1)
                nc.gpsimd.tensor_tensor((mq_nat, mk_nat)[n // NT][:, t, :], rt1[:, n % 2, :], rt2[:, n % 2, :],
                                        ALU.add).then_inc(roped, 1)
            for t in range(NT):
                rms(3, t, D, 2, 3 * NT + 3 * t + 2)
                rms(4, t, D, 1, 3 * NT + 3 * t + 3)
            for t in range(NT):
                rms(5, t, D, 2, 6 * NT + 2 * t + 2)

        @block.scalar
        def _(act):
            SLOT_LEFT = {2: (w_used, 1), 3: (proj, NT), 4: (w_used, 2), 5: (proj, 2 * NT), 6: (w_used, 3),
                         8: (qup, 2 * NT), 9: (proj, 3 * NT), 10: (w_used, 4), 11: (proj, 4 * NT),
                         12: (w_used, 5), 13: (w_used, 6), 14: (y_full, NT)}

            def split_hi(r, n, hi):
                act.wait_ge(raw_in[r % 2], 16 * (r // 2 + 1))
                if r >= 2:
                    act.wait_ge(*SLOT_LEFT[r])
                nc.scalar.copy(hi[:, 0:n], raw[r % 2][:, 0:n]).then_inc(wh_ready, 1)

            def in_hi(i):
                split_hi(IN_CH[i], 4 * GROUP_COLS[i // 2][1], w_hi[IN_CH[i] % 2])

            def square(src, norm, t, col, junk):
                nc.scalar.activation(junk, src, ACT.Square, accum_out=stat[:, norm, t, col:col + 1]).then_inc(sq, 1)

            def transposed_hi(n0, t):
                for b in range(2):
                    act.wait_ge(uT_full, n0 + 2 * t + b + 1)
                    nc.scalar.copy(uT_hi[:, 4 * b:4 * b + 4, P * t:P * t + P],
                                   ps[2 * t + b][:, :].rearrange("p (k n) -> p k n", k=4)).then_inc(uh, 1)

            for t in range(NT):
                act.wait_ge(x_in[t], 16)
                if t >= 2:
                    act.wait_ge(uT_full, 2 * (t - 1))
                square(h_sb[:, t, :], 0, t, 0, un[:, t % 2, :])
                if t == 1:
                    in_hi(0)
                if t >= 1:
                    transposed_hi(0, t - 1)
            transposed_hi(0, NT - 1)
            in_hi(1)
            in_hi(2)
            for t in range(NT):
                act.wait_ge(proj, t + 1)
                square(ps[t][:, 0:QR], 1, t, 0, cn[:, t, 0:QR])
                square(ps[t][:, QR:QR + KVR], 2, t, 0, cn[:, t, QR:])
                nc.scalar.copy(kr[:, t, :], ps[t][:, QR + KVR:CA]).then_inc(kr_c, 1)
            in_hi(3)
            in_hi(4)
            for j in range(3):
                act.wait_ge(cT_full, j + 1)
                nc.scalar.copy(cT_hi[:, j, :], ps[j][:, :]).then_inc(ch, 1)
            act.wait_ge(krT_full, 1)
            nc.scalar.copy(kT[0][NOPE:QH, :], ps[3][0:ROPE, :]).then_inc(krT_c, 1)
            nc.scalar.copy(kT[1][NOPE:QH, :], ps[3][0:ROPE, :]).then_inc(krT_c, 1)
            in_hi(5)
            split_hi(Q_CH, 2 * HEADS * QH, w_hi[Q_CH % 2])
            act.wait_ge(raw_in[KV_CH % 2], 16 * (KV_CH // 2 + 1))
            nc.scalar.copy(wkv_hi[:, :], raw[KV_CH % 2][:, 0:HEADS * P]).then_inc(wh_ready, 1)
            for n in range(2 * NT):
                act.wait_ge(qup, n + 1)
                nc.scalar.copy(q_nat[:, n // 2, 4 * QH * (n % 2):4 * QH * (n % 2 + 1)],
                               ps[n][:, 0:4 * QH]).then_inc(qup_c, 1)
                if n == 3:
                    in_hi(6)
            for t in range(NT):
                act.wait_ge(vup, t + 1)
                nc.scalar.copy(v_sb[:, 0, t, :], ps[t][:, :]).then_inc(v_ready, 1)
            in_hi(7)
            for t in range(NT):
                act.wait_ge(proj, 3 * NT + t + 1)
                nc.scalar.copy(v_sb[:, 1, t, :], ps[4 + t][:, :]).then_inc(v_ready, 1)

            def q_copy(i):
                if prepared(i):
                    act.wait_ge(qT_full, preps(i))
                    if i >= 2:
                        act.wait_ge(s_full, 3 * (before(i) + 1))
                    rows = QH if i < HEADS else P
                    nc.scalar.copy(qT[slot(i)][0:rows, :], ps[7][0:rows, :]).then_inc(qT_c, 1)

            def k_copy(i):
                if prepared(i):
                    act.wait_ge(kT_full, preps(i))
                    rows = NOPE if i < HEADS else P
                    nc.scalar.copy(kT[slot(i)][0:rows, :], ps[7][0:rows, :]).then_inc(kT_c, 1)

            def exps(i):
                act.wait_ge(s_nb, i + 1)
                if i >= 2:
                    act.wait_ge(pT_full, 3 * (i - 1))
                for t in S_ORDER:
                    b, c = S_AT[t]
                    n = P * (t + 1)
                    nc.scalar.activation(probs[i % 2][:, p_off(t):p_off(t) + n], ps[b][:, c:c + n], ACT.Exp,
                                         bias=nb[:, i % 2, t:t + 1], scale=SCALE[i],
                                         accum_out=rs[:, i % 2, t:t + 1]).then_inc(s_exp, 1)

            def pT_copy(i):
                if i >= 2:
                    act.wait_ge(o_full, i - 1)
                act.wait_ge(pT_full, 3 * i + 2)
                nc.scalar.copy(pT[i % 2][:, TOP:2 * TOP], ps[4][:, :]).then_inc(pT_act, 1)
                act.wait_ge(pT_full, 3 * i + 3)
                nc.scalar.copy(pT[i % 2][:, 2 * TOP:], ps[5][:, 0:2 * P]).then_inc(pT_act, 1)

            def o_split(i):
                act.wait_ge(o_full, i + 1)
                r0 = VD * (i % 2)
                nc.scalar.copy(uT_hi[r0:r0 + VD, i // 2, :], ps[6][0:VD, :]).then_inc(o_hi, 1)

            for i in (0, 1):
                q_copy(i)
                k_copy(i)
            exps(0)
            for i in range(NH):
                q_copy(i + 2)
                k_copy(i + 2)
                if i + 1 < NH:
                    exps(i + 1)
                if i >= 1:
                    o_split(i - 1)
                pT_copy(i)
                if i in (9, 12):
                    split_hi(OUT_CH[(9, 12).index(i)], CW, w_hi[OUT_CH[(9, 12).index(i)] % 2])
            o_split(NH - 1)

            split_hi(OUT_CH[2], CW, w_hi[OUT_CH[2] % 2])
            split_hi(OUT_CH[3], CW, w_hi[OUT_CH[3] % 2])

            def y_squares(norm, n, t, free, value):
                act.wait_ge(y_full, n + 1)
                if free is not None:
                    act.wait_ge(free, value)
                for b in range(2):
                    square(ps[2 * t + b][:, :], norm, t, b, un[:, t % 2, TOP * b:TOP * b + TOP])

            for t in range(NT):
                y_squares(3, t, t, uT_full if t >= 2 else None, 2 * NT + 2 * (t - 1))
                if t >= 1:
                    transposed_hi(2 * NT, t - 1)
                act.wait_ge(h_ready, t + 1)
                square(h_sb[:, t, :], 4, t, 0, un[:, t % 2, :])
            transposed_hi(2 * NT, NT - 1)

            def mlp_hi(j, r):
                act.wait_ge(raw_in[j], (r - j) * 8 + 16)
                nc.scalar.copy(w_hi[j][:, :], raw[j][:, :]).then_inc(wh_ready, 1)

            def up_step(i):
                for j in range(2):
                    if not (isinstance(i, int) and j == 0):
                        act.wait_ge(up_full, i * 4 + 2 * j)
                    mlp_hi(1 - j, i * 2 + (UP_CH + j + 1))
                    for m in range(2):
                        act.wait_ge(up_full, i * 4 + (2 * j + m + 1))
                        if not (isinstance(i, int) and j == 0):
                            act.wait_ge(a_ready, i * 4 + (2 * j + m - 1))
                        nc.scalar.activation(relu[:, m, :], ps[2 * j + m][:, :], ACT.Relu).then_inc(relu_c, 1)

            act.wait_ge(*SLOT_LEFT[UP_CH])
            mlp_hi(0, UP_CH)
            up_step(0)
            with act.Fori(1, NF // 4) as i:
                up_step(i)

            def down_hi(j, c):
                mlp_hi(j, c + DOWN_CH)
                nc.scalar.copy(a_hi[j][:, :, :], act_sb[:, bass.ds(c * 2, 2), :]).then_inc(ah, 1)

            act.wait_ge(a_ready, NF)
            nc.scalar.copy(a_hi[0][:, :, :], act_sb[:, 0:2, :]).then_inc(ah, 1)
            act.wait_ge(up_full, NF)
            down_hi(1, 1)
            with act.Fori(1, NF // 4) as i:
                for j in range(2):
                    act.wait_ge(w_used, i * 2 + (j - 1 + 6))
                    down_hi(j, i * 2 + j)
            for t in range(NT):
                y_squares(5, NT + t, t, h_ready if t >= 2 else None, NT + t - 1)

        @block.vector
        def _(dve):
            own = [0]

            def step(ins):
                own[0] += 1
                ins.then_inc(dve_step, 1)
                dve.wait_ge(dve_step, own[0])

            def lo_part(out, whole, hi):
                return nc.vector.tensor_tensor(out, whole, hi.bitcast(F32), ALU.subtract)

            def split_lo(r, n, hi, lo):
                dve.wait_ge(wh_ready, r + 1)
                lo_part(lo[:, 0:n], raw[r % 2][:, 0:n], hi[:, 0:n]).then_inc(w_ready, 1)

            def in_lo(i):
                r = IN_CH[i]
                split_lo(r, 4 * GROUP_COLS[i // 2][1], w_hi[r % 2], w_lo[r % 2])

            def ring_lo(r):
                split_lo(r, CW, w_hi[r % 2], w_lo[r % 2])

            def transposed_lo(n0, t):
                for b in range(2):
                    dve.wait_ge(uh, n0 + 2 * t + b + 1)
                    sl = (slice(None), slice(4 * b, 4 * b + 4), slice(P * t, P * t + P))
                    lo_part(uT_lo[sl], ps[2 * t + b][:, :].rearrange("p (k n) -> p k n", k=4), uT_hi[sl]).then_inc(ul, 1)

            def normed(norm, t, n_rstd, n_g):
                dve.wait_ge(g_pre_in, n_g)
                dve.wait_ge(rstd, n_rstd)
                nc.vector.scalar_tensor_tensor(out=un[:, t % 2, :], in0=h_sb[:, t, :], scalar=stat[:, norm, t, 3:4],
                                               in1=pre_g[:, :], op0=ALU.mult, op1=ALU.mult).then_inc(un_ready, 1)

            for t in range(NT):
                normed(0, t, t + 1, 16)
                if t == 1:
                    in_lo(0)
                if t >= 1:
                    transposed_lo(0, t - 1)
            transposed_lo(0, NT - 1)
            in_lo(1)
            in_lo(2)
            dve.wait_ge(lat_in, 32)
            for t in range(NT):
                dve.wait_ge(kr_c, t + 1)
                for norm, c0, n in ((1, 0, QR), (2, QR, KVR)):
                    dve.wait_ge(rstd, NT + 2 * t + norm)
                    nc.vector.scalar_tensor_tensor(out=cn[:, t, c0:c0 + n], in0=ps[t][:, c0:c0 + n],
                                                   scalar=stat[:, norm, t, 3:4], in1=lat_g[:, c0:c0 + n],
                                                   op0=ALU.mult, op1=ALU.mult).then_inc(cn_ready, 1)
            in_lo(3)
            dve.wait_ge(tab_in, 16)
            cosM, sinM = rope_sb[:, :, 0:32], rope_sb[:, :, 32:96]
            cosL, sinL = rope_sb[:, :, 96:112], rope_sb[:, :, 112:144]

            def pairs(a, d):
                return a.rearrange("p t (s d) -> p t s d", s=2, d=d)

            k4 = pairs(kr[:, :, :], 16)
            m1 = rt1[:, 0, 0:NT * ROPE].rearrange("p (t s d) -> p t s d", t=NT, s=2)
            m2 = rt2[:, 0, 0:NT * ROPE].rearrange("p (t s d) -> p t s d", t=NT, s=2)
            nc.vector.tensor_tensor(m1, k4, cosL.unsqueeze(2).to_broadcast([P, NT, 2, 16]), ALU.mult)
            nc.vector.tensor_tensor(m2[:, :, 0, :], k4[:, :, 1, :], sinL[:, :, 0:16], ALU.mult)
            step(nc.vector.tensor_tensor(m2[:, :, 1, :], k4[:, :, 0, :], sinL[:, :, 16:32], ALU.mult))
            nc.vector.tensor_tensor(pairs(krr[:, :, :], 16), m1, m2, ALU.add).then_inc(krr_ready, 1)
            dve.wait_ge(krr_ready, 1)

            def rotate(n):
                t, group = n % NT, 1 + n // NT
                dve.wait_ge(proj, NT * group + t + 1)
                if n >= 2:
                    dve.wait_ge(roped, n - 1)
                src = ps[4 + t][:, :].rearrange("p (h s d) -> p h s d", h=HEADS, s=2)
                o1 = rt1[:, n % 2, :].rearrange("p (g d) -> p g d", d=32)
                o2 = rt2[:, n % 2, :].rearrange("p (h s d) -> p h s d", h=HEADS, s=2)
                nc.vector.tensor_tensor(o1, ps[4 + t][:, :].rearrange("p (g d) -> p g d", d=32),
                                        cosM[:, t, :].unsqueeze(1).to_broadcast([P, 2 * HEADS, 32]), ALU.mult)
                for s in range(2):
                    last = nc.vector.tensor_tensor(o2[:, :, s, :], src[:, :, 1 - s, :],
                                                   sinM[:, t, 32 * s:32 * s + 32].unsqueeze(1).to_broadcast([P, HEADS, 32]),
                                                   ALU.mult)
                last.then_inc(rope_m, 1)

            in_lo(4)
            for t in range(NT):
                rotate(t)
            for j in range(3):
                dve.wait_ge(ch, j + 1)
                lo_part(cT_lo[:, j, :], ps[j][:, :], cT_hi[:, j, :]).then_inc(cl, 1)
            in_lo(5)
            split_lo(Q_CH, 2 * HEADS * QH, w_hi[Q_CH % 2], w_lo[Q_CH % 2])
            split_lo(KV_CH, HEADS * P, wkv_hi, wkv_lo)
            for t in range(NT):
                rotate(NT + t)
            dve.wait_ge(roped, 2 * NT)
            for t in range(NT):
                dve.wait_ge(qup_c, 2 * t + 2)
                q4 = q_nat[:, t, :].rearrange("p (h c) -> p h c", c=QH)[:, :, NOPE:QH].rearrange("p h (s d) -> p h s d", s=2)
                m1 = rt1[:, t % 2, 0:HEADS * ROPE].rearrange("p (h s d) -> p h s d", h=HEADS, s=2)
                m2 = rt2[:, t % 2, 0:HEADS * ROPE].rearrange("p (h s d) -> p h s d", h=HEADS, s=2)
                cs = cosL[:, t, :].unsqueeze(1).unsqueeze(1).to_broadcast([P, HEADS, 2, 16])
                nc.vector.tensor_tensor(m1, q4, cs, ALU.mult)
                for s in range(2):
                    last = nc.vector.tensor_tensor(m2[:, :, s, :], q4[:, :, 1 - s, :],
                                                   sinL[:, t, 16 * s:16 * s + 16].unsqueeze(1).to_broadcast([P, HEADS, 16]),
                                                   ALU.mult)
                step(last)
                nc.vector.tensor_tensor(q4, m1, m2, ALU.add).then_inc(q_roped, 1)
                if t == 1:
                    in_lo(6)
            in_lo(7)

            def maxes(i):
                for n, t in enumerate(S_ORDER):
                    b, c = S_AT[t]
                    dve.wait_ge(s_full, 3 * i + min(n + 1, 3))
                    last = nc.vector.reduce_max(mx[:, i % 2, t:t + 1], ps[b][:, c:c + P * (t + 1)], AX_X)
                step(last)
                nc.vector.tensor_scalar(nb[:, i % 2, :], mx[:, i % 2, :], -SCALE[i], None, ALU.mult).then_inc(s_nb, 1)

            def divide(i):
                dve.wait_ge(s_exp, NT * (i + 1))
                step(nc.vector.reciprocal(ri[:, i % 2, :], rs[:, i % 2, :]))
                for t in range(NT):
                    pr = probs[i % 2][:, p_off(t):p_off(t) + P * (t + 1)]
                    nc.vector.tensor_scalar(pr, pr, ri[:, i % 2, t:t + 1], None, ALU.mult).then_inc(s_norm, 1)

            def pT_copy(i):
                if i >= 2:
                    dve.wait_ge(o_full, i - 1)
                dve.wait_ge(pT_full, 3 * i + 1)
                nc.vector.tensor_copy(pT[i % 2][:, 0:TOP], ps[3][:, :]).then_inc(pT_dve, 1)

            def o_split(i):
                dve.wait_ge(o_hi, i + 1)
                r0 = VD * (i % 2)
                lo_part(uT_lo[r0:r0 + VD, i // 2, :], ps[6][0:VD, :], uT_hi[r0:r0 + VD, i // 2, :]).then_inc(o_lo, 1)

            maxes(0)
            divide(0)
            for i in range(NH):
                if i + 1 < NH:
                    maxes(i + 1)
                if i >= 1:
                    o_split(i - 1)
                pT_copy(i)
                if i + 1 < NH:
                    divide(i + 1)
                if i in (9, 12):
                    ring_lo(OUT_CH[(9, 12).index(i)])
            o_split(NH - 1)
            ring_lo(OUT_CH[2])
            ring_lo(OUT_CH[3])

            def scaled(norm, t, n_rstd, n_g):
                dve.wait_ge(g_post_in, n_g)
                dve.wait_ge(rstd, n_rstd)
                for b in range(2):
                    last = nc.vector.scalar_tensor_tensor(
                        out=un[:, t % 2, TOP * b:TOP * b + TOP], in0=ps[2 * t + b][:, :], scalar=stat[:, norm, t, 3:4],
                        in1=post_g[:, TOP * b:TOP * b + TOP], op0=ALU.mult, op1=ALU.mult)
                    last.then_inc(y_s, 1)
                scaled_n[0] += 2
                dve.wait_ge(y_s, scaled_n[0])
                nc.vector.tensor_tensor(h_sb[:, t, :], h_sb[:, t, :], un[:, t % 2, :], ALU.add).then_inc(h_ready, 1)

            scaled_n = [0]
            for t in range(NT):
                scaled(3, t, 3 * NT + 2 * t + 1, 16)
                normed(4, t, 3 * NT + 2 * t + 2, 32)
                if t >= 1:
                    transposed_lo(2 * NT, t - 1)
            transposed_lo(2 * NT, NT - 1)

            def mlp_lo(j, r):
                dve.wait_ge(wh_ready, r + 1)
                lo_part(w_lo[j][:, :], raw[j][:, :], w_hi[j][:, :]).then_inc(w_ready, 1)

            def up_step(i):
                for j in range(2):
                    mlp_lo(1 - j, i * 2 + (UP_CH + j + 1))
                    for m in range(2):
                        dve.wait_ge(relu_c, i * 4 + (2 * j + m + 1))
                        nc.vector.tensor_tensor(act_sb[:, bass.ds(i * 4 + (2 * j + m), 1), :], relu[:, m:m + 1, :],
                                                relu[:, m:m + 1, :], ALU.mult).then_inc(a_ready, 1)

            mlp_lo(0, UP_CH)
            with dve.Fori(0, NF // 4) as i:
                up_step(i)

            def down_a(j, c):
                dve.wait_ge(ah, c + 1)
                lo_part(a_lo[j][:, :, :], act_sb[:, bass.ds(c * 2, 2), :], a_hi[j][:, :, :]).then_inc(al, 1)

            def down_lo(j, c):
                mlp_lo(j, c + DOWN_CH)
                down_a(j, c)

            down_a(0, 0)
            with dve.Fori(0, NF // 4 - 1) as i:
                down_lo(1, i * 2 + 1)
                down_lo(0, i * 2 + 2)
            down_lo(1, NF // 2 - 1)
            for t in range(NT):
                scaled(5, t, 5 * NT + t + 1, 32)

        @block.tensor
        def _(pe):
            def mm3(out, lh, ll, rh, rl, start, stop):
                nc.tensor.matmul(out, lh, rh, start=start, stop=False)
                nc.tensor.matmul(out, lh, rl, start=False, stop=False)
                return nc.tensor.matmul(out, ll, rh, start=False, stop=stop)

            def transposes(n0, t):
                pe.wait_ge(un_ready, n0 // 2 + t + 1)
                for k in range(ND):
                    last = nc.tensor.transpose(ps[2 * t + k // 4][:, P * (k % 4):P * (k % 4) + P],
                                               un[:, t % 2, P * k:P * k + P], ident[:, :])
                    if k % 4 == 3:
                        last.then_inc(uT_full, 1)

            def group(g, before_tile):
                n = GROUP_COLS[g][1]
                for part in range(2):
                    r = IN_CH[2 * g + part]
                    pe.wait_ge(w_ready, r + 1)
                    for t in range(NT):
                        if part == 0:
                            before_tile(t)
                        tok = slice(P * t, P * t + P)
                        for k in range(4):
                            w = slice(n * k, n * k + n)
                            last = mm3(ps[4 * (g > 0) + t][:, 0:n], uT_hi[:, 4 * part + k, tok], uT_lo[:, 4 * part + k, tok],
                                       w_hi[r % 2][:, w], w_lo[r % 2][:, w], part == 0 and k == 0, part == 1 and k == 3)
                        if part == 1:
                            last.then_inc(proj, 1)
                    if part == 0:
                        last.then_inc(w_used, 1)

            pe.wait_ge(cst, 3)
            transposes(0, 0)
            transposes(0, 1)
            transposes(0, 2)
            transposes(0, 3)
            group(0, lambda t: pe.wait_ge(ul, 2 * t + 2))
            group(1, lambda t: None)
            pe.wait_ge(cn_ready, 2 * NT)
            for j in range(3):
                for t in range(NT):
                    last = nc.tensor.transpose(ps[j][:, P * t:P * t + P], cn[:, t, P * j:P * j + P], ident[:, :])
                last.then_inc(cT_full, 1)
            pe.wait_ge(krr_ready, 1)
            for t in range(NT):
                last = nc.tensor.transpose(ps[3][0:ROPE, P * t:P * t + P], krr[:, t, :], ident[:, :])
            last.then_inc(krT_full, 1)
            group(2, lambda t: pe.wait_ge(rope_m, t + 1))
            pe.wait_ge(w_ready, Q_CH + 1)
            pe.wait_ge(cl, 3)
            pe.wait_ge(krT_c, 2)
            for n in range(2 * NT):
                t, hf = n // 2, n % 2
                if n >= NT:
                    pe.wait_ge(rope_m, n + 1)
                for k in range(2):
                    w = slice(HEADS * QH * k + 4 * QH * hf, HEADS * QH * k + 4 * QH * (hf + 1))
                    last = mm3(ps[n][:, 0:4 * QH], cT_hi[:, k, P * t:P * t + P], cT_lo[:, k, P * t:P * t + P],
                               w_hi[Q_CH % 2][:, w], w_lo[Q_CH % 2][:, w], k == 0, k == 1)
                last.then_inc(qup, 1)
            pe.wait_ge(w_ready, KV_CH + 1)
            wv_hi = wkv_hi[:, :].rearrange("p (h c) -> p h c", c=P)[:, :, NOPE:]
            wv_lo = wkv_lo[:, :].rearrange("p (h c) -> p h c", c=P)[:, :, NOPE:]
            for t in range(NT):
                pe.wait_ge(qup_c, t + 1)
                last = mm3(ps[t][:, :].rearrange("p (h c) -> p h c", c=VD), cT_hi[:, 2, P * t:P * t + P],
                           cT_lo[:, 2, P * t:P * t + P], wv_hi, wv_lo, True, True)
                last.then_inc(vup, 1)
            group(3, lambda t: pe.wait_ge(qup_c, NT + t + 1))

            def q_prep(i):
                if prepared(i):
                    if i == 0:
                        pe.wait_ge(v_ready, 2 * NT)
                        pe.wait_ge(q_roped, NT)
                        pe.wait_ge(roped, 2 * NT)
                    else:
                        pe.wait_ge(kT_c, preps(i) - 1)
                    rows = QH if i < HEADS else P
                    src, c0 = (q_nat, QH * i) if i < HEADS else (mq_nat, MOBA_D * (i - HEADS))
                    for t in range(NT):
                        last = nc.tensor.transpose(ps[7][0:rows, P * t:P * t + P], src[:, t, c0:c0 + rows], ident[:, :])
                    last.then_inc(qT_full, 1)

            def k_prep(i):
                if prepared(i):
                    pe.wait_ge(qT_c, preps(i))
                    if i < HEADS:
                        w = slice(P * i, P * i + P)
                        last = mm3(ps[7][:, :], wkv_hi[:, w], wkv_lo[:, w], cT_hi[:, 2, :], cT_lo[:, 2, :], True, True)
                    else:
                        c0 = MOBA_D * (i - HEADS)
                        for t in range(NT):
                            last = nc.tensor.transpose(ps[7][:, P * t:P * t + P], mk_nat[:, t, c0:c0 + P], ident[:, :])
                    last.then_inc(kT_full, 1)

            def scores(i):
                pe.wait_ge(kT_c, preps(i))
                r = slice(0, QH) if i < HEADS else slice(MOBA_D * (i % 2), MOBA_D * (i % 2) + MOBA_D)
                for n, t in enumerate(S_ORDER):
                    b, c = S_AT[t]
                    if i >= 1:
                        pe.wait_ge(s_exp, NT * (i - 1) + (n + 1 if n < 2 else NT))
                    w = P * (t + 1)
                    nc.tensor.matmul(ps[b][:, c:c + w], qT[slot(i)][r, P * t:P * t + P], kT[slot(i)][r, 0:w],
                                     start=True, stop=False)
                    last = nc.tensor.matmul(ps[b][:, c + w - P:c + w], ident_b[:, :], mask_b[:, :], start=False, stop=True)
                    if n != 2:
                        last.then_inc(s_full, 1)

            def probs_T(i):
                pe.wait_ge(s_norm, NT * (i + 1))
                for k in PT_ORDER:
                    b, c = PT_AT[k]
                    if i >= 1 and k == 0:
                        pe.wait_ge(pT_dve, i)
                    if i >= 1 and k in (1, 2):
                        pe.wait_ge(pT_act, 2 * (i - 1) + (1 if k == 1 else 2))
                    for t in range(k, NT):
                        last = nc.tensor.transpose(ps[b][:, c + P * (t - k):c + P * (t - k) + P],
                                                   probs[i % 2][:, p_off(t) + P * k:p_off(t) + P * k + P], ident[:, :])
                    if k != 1:
                        last.then_inc(pT_full, 1)

            def weighted(i):
                pe.wait_ge(pT_dve, i + 1)
                pe.wait_ge(pT_act, 2 * (i + 1))
                if i >= 1:
                    pe.wait_ge(o_lo, i)
                h = i % HEADS
                for k in range(NT):
                    last = nc.tensor.matmul(ps[6][0:VD, P * k:TOP], v_sb[:, i // HEADS, k, VD * h:VD * h + VD],
                                            pT[i % 2][:, PT_OFF[k]:PT_OFF[k] + P * (NT - k)], start=k == 0, stop=k == NT - 1)
                last.then_inc(o_full, 1)

            for i in (0, 1):
                q_prep(i)
                k_prep(i)
            scores(0)
            for i in range(NH):
                q_prep(i + 2)
                if i + 1 < NH:
                    scores(i + 1)
                k_prep(i + 2)
                if i >= 1:
                    weighted(i - 1)
                probs_T(i)
            weighted(NH - 1)

            def two_rows(t, l_hi, l_lo, j, kk, start, stop):
                for b in range(2):
                    w = slice(D * kk + TOP * b, D * kk + TOP * b + TOP)
                    last = mm3(ps[2 * t + b][:, :], l_hi, l_lo, w_hi[j][:, w], w_lo[j][:, w], start, stop)
                return last

            pe.wait_ge(o_lo, NH)
            def out_rows(t, c, kk):
                tok, k = slice(P * t, P * t + P), 2 * c + kk
                return two_rows(t, uT_hi[:, k, tok], uT_lo[:, k, tok], OUT_CH[c] % 2, kk, k == 0, k == ND - 1)

            for c in range(2):
                pe.wait_ge(w_ready, OUT_CH[c] + 1)
                for t in range(NT):
                    for kk in range(2):
                        last = out_rows(t, c, kk)
                last.then_inc(w_used, 1)
            pe.wait_ge(w_ready, OUT_CH[3] + 1)
            for t in range(NT):
                for c in (2, 3):
                    for kk in range(2):
                        last = out_rows(t, c, kk)
                last.then_inc(y_full, 1)
                if t >= 1:
                    pe.wait_ge(y_s, 2 * t)
                    transposes(2 * NT, t - 1)
            transposes(2 * NT, NT - 1)

            def up_step(i):
                for j in range(2):
                    pe.wait_ge(w_ready, i * 2 + (UP_CH + j + 1))
                    for m in range(2):
                        if not isinstance(i, int):
                            pe.wait_ge(relu_c, i * 4 + (2 * j + m - 3))
                        for k in range(ND):
                            w = slice(256 * k + P * m, 256 * k + P * m + P)
                            whi, wlo = w_hi[j][:, w], w_lo[j][:, w]
                            last = mm3(ps[2 * j + m][:, :], whi, wlo, uT_hi[:, k, :], uT_lo[:, k, :], k == 0, k == ND - 1)
                        last.then_inc(up_full, 1)

            pe.wait_ge(ul, 4 * NT)
            up_step(0)
            with pe.Fori(1, NF // 4) as i:
                up_step(i)

            def down_rows(t, j, kk, start, stop):
                tok = slice(P * t, P * t + P)
                return two_rows(t, a_hi[j][:, kk, tok], a_lo[j][:, kk, tok], j, kk, start, stop)

            def down_chunk(j, c, first=False):
                pe.wait_ge(w_ready, c + (DOWN_CH + 1))
                pe.wait_ge(al, c + 1)
                for t in range(NT):
                    for kk in range(2):
                        last = down_rows(t, j, kk, first and kk == 0, False)
                last.then_inc(w_used, 1)

            pe.wait_ge(relu_c, NF)
            down_chunk(0, 0, True)
            down_chunk(1, 1)
            with pe.Fori(1, NF // 4 - 1) as i:
                down_chunk(0, i * 2)
                down_chunk(1, i * 2 + 1)
            pe.wait_ge(w_ready, DOWN_CH + NF // 2)
            pe.wait_ge(al, NF // 2)
            for t in range(NT):
                for j in range(2):
                    for kk in range(2):
                        last = down_rows(t, j, kk, False, j == 1 and kk == 1)
                last.then_inc(y_full, 1)


def rope_constants(seq):
    import numpy as np

    cols = []
    for half in (MOBA_D // 2, ROPE // 2):
        inv = (np.float32(1.0) / np.float32(10000.0) ** (np.arange(half, dtype=np.float32) / np.float32(half))).astype(np.float32)
        ang = (np.arange(seq, dtype=np.float32)[:, None] * inv[None, :]).astype(np.float32)
        c, s = np.cos(ang).astype(np.float32), np.sin(ang).astype(np.float32)
        cols += [c, -s, s]
    return np.ascontiguousarray(np.concatenate(cols, axis=1))


NAMES = ["x", "attn_pre_g", "w_in", "mla_q_norm_g", "w_mla_q_up", "mla_kv_norm_g", "w_mla_kv_up", "w_out",
         "attn_post_g", "mlp_pre_g", "w_up", "w_down", "mlp_post_g"]


def kernel(**inputs):
    import numpy as np
    import concourse.bacc as bacc
    from concourse.bass_utils import run_bass_kernel_spmd

    nc = bacc.Bacc("TRN2", target_bir_lowering=False, num_devices=1)
    arrays = {name: np.ascontiguousarray(inputs[name]) for name in NAMES}
    arrays["rope_table"] = rope_constants(arrays["x"].shape[1])
    args = [nc.dram_tensor(f"in_{name}", a.shape, mybir.dt.from_np(a.dtype), kind="ExternalInput").ap()
            for name, a in arrays.items()]
    out = nc.dram_tensor("out", arrays["x"].shape, F32, kind="ExternalOutput").ap()
    build(nc, *args, out)
    r = run_bass_kernel_spmd(nc, [{f"in_{name}": a for name, a in arrays.items()}], core_ids=[0])
    return r.results[0]["out"]
```

```python
from contextlib import ExitStack

import concourse.bass as bass
from concourse import mybir

F32 = mybir.dt.float32
F32R = mybir.dt.float32r
BF16 = mybir.dt.bfloat16
ALU = mybir.AluOpType
ACT = mybir.ActivationFunctionType
AX_X = mybir.AxisListType.X

P = 128
EPS = 1e-6
NEG = -1e30
NOPE, ROPE, VD = 64, 32, 64
HEADS = 8
MOBA_D = 64
TOP = 512


def build(nc, x, attn_pre_g, w_in, mla_q_norm_g, w_mla_q_up, mla_kv_norm_g, w_mla_kv_up, w_out,
          attn_post_g, mlp_pre_g, w_up, w_down, mlp_post_g, rope_table, out):
    S, D = x.shape[1], x.shape[2]
    F = w_up.shape[2]
    QR, KVR = w_mla_q_up.shape[1], w_mla_kv_up.shape[1]
    NT = S // P
    ND = D // P
    NF = F // P
    CA = QR + KVR + ROPE
    HW = HEADS * MOBA_D
    QH = NOPE + ROPE
    CW = 2048
    NH = 2 * HEADS
    SCALE = [float(QH) ** -0.5] * HEADS + [float(MOBA_D) ** -0.5] * HEADS
    assert (S, D, F, NT, CA) == (512, 1024, 4096, 4, 416)

    x_v = x[0].rearrange("(t p) d -> t p d", p=P)
    out_v = out[0].rearrange("(t p) d -> t p d", p=P)
    w_in_v = w_in[0].rearrange("(k p) n -> p k n", p=P)
    w_q_v = w_mla_q_up[0].rearrange("(k p) n -> p k n", p=P)
    w_out_v = w_out[0].rearrange("(k p) n -> p k n", p=P)
    w_up_v = w_up[0].rearrange("(k p) n -> p k n", p=P)
    w_down_v = w_down[0].rearrange("(k p) n -> p k n", p=P)

    IN_CH = [0, 1, 2, 3, 4, 5, 8, 9]
    Q_CH, KV_CH = 6, 7
    OUT_CH = [10, 11, 12, 13]
    UP_CH = 14
    DOWN_CH = UP_CH + NF // 2
    NO = len(OUT_CH)
    GROUP_COLS = [(0, CA), (CA, HW), (CA + HW, HW), (CA + 2 * HW, HW)]
    TRI = NT * (NT + 1) // 2 * P

    with ExitStack() as ctx:
        def sb(name, shape, dt=F32, stack=ctx):
            return stack.enter_context(nc.sbuf_tensor(name, shape, dt))

        def sem(name):
            return ctx.enter_context(nc.semaphore(name))

        uT_hi = sb("uT_hi", [P, ND, S], F32R)
        uT_lo = sb("uT_lo", [P, ND, S], F32R)
        raw = [sb(f"w_raw{i}", [P, CW]) for i in range(2)]
        w_hi = [sb(f"w_hi{i}", [P, CW], F32R) for i in range(2)]
        w_lo = [sb(f"w_lo{i}", [P, CW], F32R) for i in range(2)]
        g_in = sb("g_in", [P, ND])
        g_up = sb("g_up", [P, ND])
        ident = sb("ident", [P, P])
        ident_b = sb("ident_b", [P, P], BF16)
        mask_b = sb("mask_b", [P, P], BF16)
        half = sb("half", [P, 1])
        stat = sb("stat", [P, 6, NT, 4])
        junk = sb("junk", [P, D], BF16)
        att = ExitStack()
        with ExitStack() as mla:
            cT_hi = sb("cT_hi", [P, 3, S], F32R, stack=mla)
            cT_lo = sb("cT_lo", [P, 3, S], F32R, stack=mla)
            wkv_hi = sb("wkv_hi", [P, HEADS * P], F32R, stack=mla)
            wkv_lo = sb("wkv_lo", [P, HEADS * P], F32R, stack=mla)
            q_nat = sb("q_nat", [P, NT, HEADS * QH], stack=mla)
        wo_hi = [sb(f"wo_hi{i}", [P, CW], F32R, stack=att) for i in range(2)]
        wo_lo = [sb(f"wo_lo{i}", [P, CW], F32R, stack=att) for i in range(2)]
        mq_nat = sb("mq_nat", [P, NT, HW], stack=att)
        mk_nat = sb("mk_nat", [P, NT, HW], stack=att)
        with ExitStack() as start:
            x_sb = sb("x_sb", [P, NT, D], stack=start)
        v_hi = sb("v_hi", [P, 2, NT, HW], F32R, stack=att)
        v_lo = sb("v_lo", [P, 2, NT, HW], F32R, stack=att)
        qT_hi = [sb(f"qT_hi{i}", [P, S], F32R, stack=att) for i in range(2)]
        qT_lo = [sb(f"qT_lo{i}", [P, S], F32R, stack=att) for i in range(2)]
        kT_hi = [sb(f"kT_hi{i}", [P, S], F32R, stack=att) for i in range(2)]
        kT_lo = [sb(f"kT_lo{i}", [P, S], F32R, stack=att) for i in range(2)]
        mx = sb("mx", [P, 2, NT], stack=att)
        nb = sb("nb", [P, 2, NT], stack=att)
        rs = sb("rs", [P, 2, NT], stack=att)
        ri = sb("ri", [P, 2, NT], stack=att)
        with ExitStack() as pre:
            lat_g = sb("lat_g", [P, QR + KVR], stack=pre)
            rope_sb = sb("rope_sb", [P, NT, rope_table.shape[1]], stack=pre)
            cn = sb("cn", [P, NT, QR + KVR], stack=pre)
            kr = sb("kr", [P, NT, ROPE], stack=pre)
            krr = sb("krr", [P, NT, ROPE], stack=pre)
            rt1 = sb("rt1", [P, 2, HW], stack=pre)
            rt2 = sb("rt2", [P, 2, HW], stack=pre)
        probs = [sb(f"probs{i}", [P, TRI], stack=att) for i in range(2)]
        pT_hi = sb("pT_hi", [P, TRI], F32R, stack=att)
        pT_lo = sb("pT_lo", [P, TRI], F32R, stack=att)
        att.close()
        act_sb = sb("act_sb", [P, NF, S])
        h_sb = sb("h_sb", [P, NT, D])
        relu = sb("relu", [P, 2, S])
        a_hi = [sb(f"a_hi{i}", [P, 2, S], F32R) for i in range(2)]
        a_lo = [sb(f"a_lo{i}", [P, 2, S], F32R) for i in range(2)]
        post_g = sb("post_g", [P, D])
        un = sb("un", [P, D])

        ps = [ctx.enter_context(nc.psum_tensor(f"bank{b}", [P, TOP], F32)) for b in range(8)]

        x_in = [sem(f"x{t}_in") for t in range(NT)]
        h_in = [sem(f"h{t}_in") for t in range(NT)]
        g_in_in, g_up_in, g_post_in = sem("g_in_in"), sem("g_up_in"), sem("g_post_in")
        tab_in, lat_in = sem("tab_in"), sem("lat_in")
        raw_in = [sem(f"raw{i}_in") for i in range(2)]
        wh_ready = sem("wh_ready")
        w_ready = sem("w_ready")
        wo_hi_ready = sem("wo_hi_ready")
        wo_ready = sem("wo_ready")
        w_used = sem("w_used")
        zeroed, consts = sem("zeroed"), sem("consts")
        sq = sem("sq")
        pool_step = sem("pool_step")
        dve_step = sem("dve_step")
        rstd = sem("rstd")
        uT_full = sem("uT_full")
        uh = sem("uh")
        ul = sem("ul")
        proj = sem("proj")
        kr_c, krr_ready = sem("kr_c"), sem("krr_ready")
        cn_ready = sem("cn_ready")
        rope_m = sem("rope_m")
        roped = sem("roped")
        cT_full, krT_full = sem("cT_full"), sem("krT_full")
        ch, cl = sem("ch"), sem("cl")
        krh, krl = sem("krh"), sem("krl")
        qup, qup_c, q_roped = sem("qup"), sem("qup_c"), sem("q_roped")
        v_full, vh, vl = sem("v_full"), sem("vh"), sem("vl")
        qT_full, qh, ql = sem("qT_full"), sem("qh"), sem("ql")
        kT_full, kh, kl = sem("kT_full"), sem("kh"), sem("kl")
        s_full, s_nb, s_exp = sem("s_full"), sem("s_nb"), sem("s_exp")
        s_ri, s_norm = sem("s_ri"), sem("s_norm")
        pT_full, ph, pl = sem("pT_full"), sem("ph"), sem("pl")
        o_full, oh, ol = sem("o_full"), sem("oh"), sem("ol")
        y_full = sem("y_full")
        y_s = sem("y_s")
        h_ready = sem("h_ready")
        up_full, relu_c, a_ready = sem("up_full"), sem("relu_c"), sem("a_ready")
        ah, al = sem("ah"), sem("al")
        out_done = sem("out_done")

        def p_off(t):
            return P * (t * (t + 1) // 2)

        PT_OFF = [0, TOP, 2 * TOP, 2 * TOP - P]

        def slot(i):
            return i % 2 if i < HEADS else (i // 2) % 2

        def before(i):
            return i - 2 if i <= HEADS else i - 3

        def prepared(i):
            return i < NH and (i < HEADS or i % 2 == 0)

        def preps(i):
            return i + 1 if i < HEADS else HEADS + (i - HEADS) // 2 + 1

        def qk_banks(i):
            return [(0, 1), (2, 3)][i] if i < 2 else (3, 7)

        S_AT = [(0, 0), (1, 0), (0, P), (2, 0)]
        S_ORDER = [3, 1, 0, 2]
        PT_AT = [(3, 0), (4, 0), (5, 0), (4, 3 * P)]
        PT_ORDER = [0, 1, 3, 2]
        PT_COPY = [(3, 0, TOP), (4, TOP, TOP), (5, 2 * TOP, 2 * P)]
        PIECE = 512
        OUT_PIECES = {i: [2 * (i - 8), 2 * (i - 8) + 1] for i in range(8, NH)}

        block = ctx.enter_context(nc.Block())

        @block.sync
        def _(sp):
            def chunk(r, src, n):
                if r - 2 in OUT_CH:
                    sp.wait_ge(wo_ready, OUT_CH.index(r - 2) + 1)
                elif r >= 2:
                    sp.wait_ge(w_ready, r - 1)
                k = src.shape[1]
                dst = raw[r % 2][:, 0:n].rearrange("p (k n) -> p k n", k=k)
                sp.dma_start(dst, src).then_inc(raw_in[r % 2], 16)

            def in_chunk(i):
                g, part = i // 2, i % 2
                c0, n = GROUP_COLS[g]
                chunk(IN_CH[i], w_in_v[:, 4 * part:4 * part + 4, c0:c0 + n], 4 * n)

            sp.dma_start(x_sb[:, 0, :], x_v[0]).then_inc(x_in[0], 16)
            in_chunk(0)
            for t in range(1, NT):
                sp.dma_start(x_sb[:, t, :], x_v[t]).then_inc(x_in[t], 16)
            in_chunk(1)
            sp.dma_start(rope_sb[:, :, :], rope_table.rearrange("(t p) c -> p t c", p=P)).then_inc(tab_in, 16)
            sp.dma_start(lat_g[:, 0:QR], mla_q_norm_g.to_broadcast([P, QR])).then_inc(lat_in, 16)
            sp.dma_start(lat_g[:, QR:], mla_kv_norm_g.to_broadcast([P, KVR])).then_inc(lat_in, 16)
            for i in range(2, 6):
                in_chunk(i)
            sp.dma_start(g_up[:, :], mlp_pre_g[0].rearrange("(k p) -> p k", p=P), allow_slow_non_contiguous=True).then_inc(g_up_in, 16)
            chunk(Q_CH, w_q_v, 2 * HEADS * QH)
            chunk(KV_CH, w_mla_kv_up.rearrange("o p n -> p o n"), HEADS * P)
            in_chunk(6)
            in_chunk(7)
            for i, r in enumerate(OUT_CH):
                chunk(r, w_out_v[:, 2 * i:2 * i + 2, :], CW)
            sp.wait_ge(o_full, NH)
            for t in range(NT):
                sp.dma_start(h_sb[:, t, :], x_v[t]).then_inc(h_in[t], 16)
            sp.dma_start(post_g[:, :], attn_post_g.to_broadcast([P, D])).then_inc(g_post_in, 16)
            for j in range(2):
                chunk(UP_CH + j, w_up_v[:, :, 256 * j:256 * j + 256], CW)
            with sp.Fori(1, NF // 4) as i:
                for j in range(2):
                    sp.wait_ge(w_ready, i * 2 + (UP_CH + j - 1 - NO))
                    sp.dma_start(raw[j][:, :].rearrange("p (k n) -> p k n", k=ND),
                                 w_up_v[:, :, bass.ds(i * 512 + j * 256, 256)]).then_inc(raw_in[j], 16)
            with sp.Fori(0, NF // 4) as i:
                for j in range(2):
                    sp.wait_ge(w_ready, i * 2 + (DOWN_CH + j - 1 - NO))
                    sp.dma_start(raw[j][:, :].rearrange("p (k n) -> p k n", k=2),
                                 w_down_v[:, bass.ds(i * 4 + 2 * j, 2), :]).then_inc(raw_in[j], 16)
            sp.wait_ge(y_s, 2 * NT)
            sp.dma_start(post_g[:, :], mlp_post_g.to_broadcast([P, D])).then_inc(g_post_in, 16)
            for n in range(2 * NT):
                t, c = n // 2, TOP * (n % 2)
                sp.wait_ge(h_ready, 2 * NT + n + 1)
                sp.dma_start(out_v[t][:, c:c + TOP], h_sb[:, t, c:c + TOP]).then_inc(out_done, 16)
            sp.wait_ge(out_done, 16 * 2 * NT)

        @block.gpsimd
        def _(pool):
            nc.gpsimd.memset(ident[:, :], 0.0).then_inc(zeroed, 1)
            nc.gpsimd.memset(ident_b[:, :], 0.0).then_inc(zeroed, 1)
            nc.gpsimd.memset(mask_b[:, :], 0.0).then_inc(zeroed, 1)
            nc.gpsimd.memset(half[:, :], -0.5).then_inc(zeroed, 1)
            pool.wait_ge(zeroed, 4)
            for m in (ident, ident_b):
                nc.gpsimd.affine_select(out=m[:, :], in_=m[:, :], compare_op=ALU.not_equal, fill=1.0, base=0,
                                        pattern=[[-1, P]], channel_multiplier=1).then_inc(consts, 1)
            nc.gpsimd.affine_select(out=mask_b[:, :], in_=mask_b[:, :], compare_op=ALU.is_ge, fill=NEG, base=0,
                                    pattern=[[-1, P]], channel_multiplier=1).then_inc(consts, 1)
            own = [0]

            def step(ins):
                own[0] += 1
                ins.then_inc(pool_step, 1)
                pool.wait_ge(pool_step, own[0])

            def rms(norm, t, n, n_sq, parts=1, by=None, squared=False):
                pool.wait_ge(sq, n_sq)
                s = stat[:, norm, t, :]
                src = s[:, 0:1]
                if parts == 2:
                    step(nc.gpsimd.tensor_tensor(s[:, 2:3], s[:, 0:1], s[:, 1:2], ALU.add))
                    src = s[:, 2:3]
                step(nc.gpsimd.tensor_scalar(s[:, 2:3], src, 1.0 / n, EPS, ALU.mult, ALU.add))
                last = nc.gpsimd.tensor_tensor(s[:, 3:4], s[:, 2:3], half[:, :], ALU.pow)
                if by is not None or squared:
                    step(last)
                    last = nc.gpsimd.tensor_tensor(s[:, 3:4], s[:, 3:4], s[:, 3:4] if squared else by, ALU.mult)
                last.then_inc(rstd, 1)

            for t in range(NT):
                rms(0, t, D, t + 1)
            for t in range(NT):
                rms(1, t, QR, NT + 2 * t + 1, by=stat[:, 0, t, 3:4])
                rms(2, t, KVR, NT + 2 * t + 2, by=stat[:, 0, t, 3:4])
            for n in range(2 * NT):
                t = n % NT
                pool.wait_ge(rope_m, n + 1)
                nc.gpsimd.tensor_tensor((mq_nat, mk_nat)[n // NT][:, t, :], rt1[:, n % 2, :], rt2[:, n % 2, :],
                                        ALU.add).then_inc(roped, 1)
            def out_piece(n):
                per = CW // PIECE
                c, w = n // per, slice(PIECE * (n % per), PIECE * (n % per) + PIECE)
                hi, lo = (w_hi[c], w_lo[c]) if c < 2 else (wo_hi[c - 2], wo_lo[c - 2])
                pool.wait_ge(wo_hi_ready, n + 1)
                last = nc.gpsimd.tensor_tensor(lo[:, w], raw[c % 2][:, w], hi[:, w].bitcast(F32), ALU.subtract)
                if n % per == per - 1:
                    last.then_inc(wo_ready, 1)

            for i in range(NH):
                for n in OUT_PIECES.get(i - 1, []):
                    out_piece(n)
                for n, t in enumerate(S_ORDER):
                    pool.wait_ge(s_ri, 2 * i + (1 if n == 0 else 2))
                    pr = probs[i % 2][:, p_off(t):p_off(t) + P * (t + 1)]
                    nc.gpsimd.tensor_tensor(pr, pr, ri[:, i % 2, t:t + 1].to_broadcast([P, P * (t + 1)]),
                                            ALU.mult).then_inc(s_norm, 1)
            for n in OUT_PIECES[NH - 1]:
                out_piece(n)
            for t in range(NT):
                rms(3, t, D, 3 * NT + 2 * t + 2, parts=2)
            for t in range(NT):
                rms(4, t, D, 5 * NT + t + 1, squared=True)
            for t in range(NT):
                rms(5, t, D, 6 * NT + 2 * t + 2, parts=2, by=stat[:, 4, t, 3:4])

        @block.scalar
        def _(act):
            act.dma_start(g_in[:, :], attn_pre_g[0].rearrange("(k p) -> p k", p=P), allow_slow_non_contiguous=True).then_inc(g_in_in, 16)

            SLOT_LEFT = {2: (w_used, 1), 3: (proj, NT), 4: (w_used, 2), 5: (proj, 2 * NT), 6: (w_used, 3),
                         8: (qup, 2 * NT), 9: (proj, 3 * NT), 10: (w_used, 4), 11: (proj, 4 * NT),
                         12: (kT_full, HEADS), 13: (kT_full, HEADS), 14: (w_used, 5), 15: (w_used, 6)}

            def arrived(r):
                act.wait_ge(raw_in[r % 2], 16 * (r // 2 + 1))
                if r in SLOT_LEFT:
                    act.wait_ge(*SLOT_LEFT[r])

            def hi_part(out, whole, scale=1.0):
                return nc.scalar.activation(out, whole, ACT.Copy, scale=scale)

            def in_hi(i):
                r, n = IN_CH[i], GROUP_COLS[i // 2][1]
                arrived(r)
                for k in range(4):
                    w, kg = slice(n * k, n * k + n), 4 * (i % 2) + k
                    last = hi_part(w_hi[r % 2][:, w], raw[r % 2][:, w], g_in[:, kg:kg + 1])
                last.then_inc(wh_ready, 1)

            squares = [0]

            def square(src, norm, t, col, scale=1.0):
                if squares[0]:
                    act.wait_ge(sq, squares[0])
                squares[0] += 1
                nc.scalar.activation(junk[:, 0:src.shape[1]], src, ACT.Square, scale=scale,
                                     accum_out=stat[:, norm, t, col:col + 1]).then_inc(sq, 1)

            def transposed_hi(n0, t):
                for b in range(2):
                    act.wait_ge(uT_full, n0 + 2 * t + b + 1)
                    hi_part(uT_hi[:, 4 * b:4 * b + 4, P * t:P * t + P],
                            ps[2 * t + b][:, :].rearrange("p (k n) -> p k n", k=4)).then_inc(uh, 1)

            transposed_hi(0, 0)
            act.wait_ge(g_in_in, 16)
            in_hi(0)
            for t in range(1, NT):
                transposed_hi(0, t)
            in_hi(1)
            for t in range(NT):
                act.wait_ge(x_in[t], 16)
                square(x_sb[:, t, :], 0, t, 0)
            in_hi(2)
            for t in range(NT):
                r = stat[:, 0, t, 3:4]
                act.wait_ge(rstd, t + 1)
                act.wait_ge(proj, t + 1)
                square(ps[t][:, 0:QR], 1, t, 0, r)
                square(ps[t][:, QR:QR + KVR], 2, t, 0, r)
                hi_part(kr[:, t, :], ps[t][:, QR + KVR:CA], r).then_inc(kr_c, 1)
            in_hi(3)
            in_hi(4)
            for j in range(3):
                act.wait_ge(cT_full, j + 1)
                hi_part(cT_hi[:, j, :], ps[j][:, :]).then_inc(ch, 1)
            act.wait_ge(krT_full, 1)
            for i in range(2):
                hi_part(kT_hi[i][NOPE:QH, :], ps[3][0:ROPE, :]).then_inc(krh, 1)
            in_hi(5)
            arrived(Q_CH)
            hi_part(w_hi[Q_CH % 2][:, 0:2 * HEADS * QH], raw[Q_CH % 2][:, 0:2 * HEADS * QH]).then_inc(wh_ready, 1)
            arrived(KV_CH)
            hi_part(wkv_hi[:, :], raw[KV_CH % 2][:, 0:HEADS * P]).then_inc(wh_ready, 1)
            for n in range(2 * NT):
                act.wait_ge(qup, n + 1)
                nc.scalar.copy(q_nat[:, n // 2, 4 * QH * (n % 2):4 * QH * (n % 2 + 1)],
                               ps[n][:, 0:4 * QH]).then_inc(qup_c, 1)
                if n == 3:
                    in_hi(6)
            for t in range(NT):
                act.wait_ge(v_full, t + 1)
                hi_part(v_hi[:, 0, t, :], ps[t][:, :]).then_inc(vh, 1)
            in_hi(7)

            def q_part(i):
                if prepared(i):
                    act.wait_ge(qT_full, preps(i))
                    if i >= 2:
                        act.wait_ge(s_full, 3 * (before(i) + 1))
                    rows = QH if i < HEADS else P
                    hi_part(qT_hi[slot(i)][0:rows, :], ps[qk_banks(i)[0]][0:rows, :]).then_inc(qh, 1)

            def k_part(i):
                if prepared(i):
                    act.wait_ge(kT_full, preps(i))
                    rows = NOPE if i < HEADS else P
                    hi_part(kT_hi[slot(i)][0:rows, :], ps[qk_banks(i)[1]][0:rows, :]).then_inc(kh, 1)

            def exps(i):
                if i >= 2:
                    act.wait_ge(pT_full, 3 * (i - 1))
                for j, t in enumerate(S_ORDER):
                    act.wait_ge(s_nb, 2 * i + (1 if j == 0 else 2))
                    b, c = S_AT[t]
                    n = P * (t + 1)
                    nc.scalar.activation(probs[i % 2][:, p_off(t):p_off(t) + n], ps[b][:, c:c + n], ACT.Exp,
                                         bias=nb[:, i % 2, t:t + 1], scale=SCALE[i],
                                         accum_out=rs[:, i % 2, t:t + 1]).then_inc(s_exp, 1)

            def p_part(i):
                if i >= 1:
                    act.wait_ge(o_full, i)
                for n, (b, c, w) in enumerate(PT_COPY):
                    act.wait_ge(pT_full, 3 * i + n + 1)
                    hi_part(pT_hi[:, c:c + w], ps[b][:, 0:w]).then_inc(ph, 1)

            def o_part(i):
                act.wait_ge(o_full, i + 1)
                r0 = VD * (i % 2)
                hi_part(uT_hi[r0:r0 + VD, i // 2, :], ps[6][0:VD, :]).then_inc(oh, 1)

            def out_piece(n):
                per = CW // PIECE
                c, w = n // per, slice(PIECE * (n % per), PIECE * (n % per) + PIECE)
                if n % per == 0:
                    arrived(OUT_CH[c])
                hi = w_hi[OUT_CH[c] % 2] if c < 2 else wo_hi[c - 2]
                hi_part(hi[:, w], raw[OUT_CH[c] % 2][:, w]).then_inc(wo_hi_ready, 1)

            for i in (0, 1):
                q_part(i)
                k_part(i)
            exps(0)
            for t in range(NT):
                act.wait_ge(proj, 3 * NT + t + 1)
                hi_part(v_hi[:, 1, t, :], ps[4 + t][:, :], stat[:, 0, t, 3:4]).then_inc(vh, 1)
            q_part(2)
            k_part(2)
            for i in range(NH + 1):
                if i >= 1:
                    p_part(i - 1)
                q_part(i + 3)
                if i + 1 < NH:
                    exps(i + 1)
                if i >= 1:
                    o_part(i - 1)
                k_part(i + 3)
                for n in OUT_PIECES.get(i, []):
                    out_piece(n)

            def mlp_hi(j, r, gains=True):
                act.wait_ge(raw_in[j], (r - j) * 8 + 16)
                if gains:
                    for k in range(ND):
                        w = slice(256 * k, 256 * k + 256)
                        last = hi_part(w_hi[j][:, w], raw[j][:, w], g_up[:, k:k + 1])
                else:
                    last = hi_part(w_hi[j][:, :], raw[j][:, :])
                last.then_inc(wh_ready, 1)

            act.wait_ge(g_up_in, 16)
            for j in range(2):
                act.wait_ge(*SLOT_LEFT[UP_CH + j])
                mlp_hi(j, UP_CH + j)

            def y_squares(norm, n, t, scale=1.0):
                for b in range(2):
                    act.wait_ge(y_full, 2 * n + b + 1)
                    square(ps[2 * t + b][:, :], norm, t, b, scale)

            for t in range(NT):
                y_squares(3, t, t)
                if t >= 1:
                    transposed_hi(2 * NT, t - 1)
            transposed_hi(2 * NT, NT - 1)
            for t in range(NT):
                square(h_sb[:, t, :], 4, t, 0)

            def up_step(i, first=False, last=False):
                for j in range(2):
                    if not (first and j == 0):
                        act.wait_ge(up_full, i * 4 + 2 * j)
                        mlp_hi(1 - j, i * 2 + (UP_CH + j + 1), not (last and j == 1))
                    for m in range(2):
                        act.wait_ge(up_full, i * 4 + (2 * j + m + 1))
                        if not (first and j == 0):
                            act.wait_ge(a_ready, i * 4 + (2 * j + m - 1))
                        nc.scalar.activation(relu[:, m, :], ps[2 * j + m][:, :], ACT.Relu).then_inc(relu_c, 1)

            up_step(0, first=True)
            act.wait_ge(a_ready, 2)
            hi_part(a_hi[0][:, :, :], act_sb[:, 0:2, :]).then_inc(ah, 1)
            with act.Fori(1, NF // 4 - 1) as i:
                up_step(i)
            up_step(NF // 4 - 1, last=True)

            def down_hi(j, c):
                mlp_hi(j, c + DOWN_CH, False)
                hi_part(a_hi[j][:, :, :], act_sb[:, bass.ds(c * 2, 2), :]).then_inc(ah, 1)

            act.wait_ge(up_full, NF)
            act.wait_ge(a_ready, NF)
            down_hi(1, 1)
            with act.Fori(1, NF // 4) as i:
                for j in range(2):
                    act.wait_ge(w_used, i * 2 + (j - 1 + 6))
                    down_hi(j, i * 2 + j)
            for t in range(NT):
                act.wait_ge(rstd, 4 * NT + t + 1)
                y_squares(5, NT + t, t, stat[:, 4, t, 3:4])

        @block.vector
        def _(dve):
            own = [0]

            def step(ins):
                own[0] += 1
                ins.then_inc(dve_step, 1)
                dve.wait_ge(dve_step, own[0])

            def lo_part(out, whole, hi):
                return nc.vector.tensor_tensor(out, whole, hi.bitcast(F32), ALU.subtract)

            def lo_scaled(out, whole, scale, hi):
                return nc.vector.scalar_tensor_tensor(out=out, in0=whole, scalar=scale, in1=hi.bitcast(F32),
                                                      op0=ALU.mult, op1=ALU.subtract)

            def in_lo(i):
                r, n = IN_CH[i], GROUP_COLS[i // 2][1]
                dve.wait_ge(wh_ready, r + 1)
                for k in range(4):
                    w, kg = slice(n * k, n * k + n), 4 * (i % 2) + k
                    last = lo_scaled(w_lo[r % 2][:, w], raw[r % 2][:, w], g_in[:, kg:kg + 1], w_hi[r % 2][:, w])
                last.then_inc(w_ready, 1)

            def transposed_lo(n0, t):
                for b in range(2):
                    dve.wait_ge(uh, n0 + 2 * t + b + 1)
                    sl = (slice(None), slice(4 * b, 4 * b + 4), slice(P * t, P * t + P))
                    lo_part(uT_lo[sl], ps[2 * t + b][:, :].rearrange("p (k n) -> p k n", k=4), uT_hi[sl]).then_inc(ul, 1)

            transposed_lo(0, 0)
            in_lo(0)
            for t in range(1, NT):
                transposed_lo(0, t)
            in_lo(1)
            in_lo(2)
            dve.wait_ge(lat_in, 32)
            for t in range(NT):
                dve.wait_ge(kr_c, t + 1)
                for norm, c0, n in ((1, 0, QR), (2, QR, KVR)):
                    dve.wait_ge(rstd, NT + 2 * t + norm)
                    nc.vector.scalar_tensor_tensor(out=cn[:, t, c0:c0 + n], in0=ps[t][:, c0:c0 + n],
                                                   scalar=stat[:, norm, t, 3:4], in1=lat_g[:, c0:c0 + n],
                                                   op0=ALU.mult, op1=ALU.mult).then_inc(cn_ready, 1)
            in_lo(3)
            dve.wait_ge(tab_in, 16)
            cosM, sinM = rope_sb[:, :, 0:32], rope_sb[:, :, 32:96]
            cosL, sinL = rope_sb[:, :, 96:112], rope_sb[:, :, 112:144]

            def pairs(a, d):
                return a.rearrange("p t (s d) -> p t s d", s=2, d=d)

            k4 = pairs(kr[:, :, :], 16)
            m1 = rt1[:, 0, 0:NT * ROPE].rearrange("p (t s d) -> p t s d", t=NT, s=2)
            m2 = rt2[:, 0, 0:NT * ROPE].rearrange("p (t s d) -> p t s d", t=NT, s=2)
            nc.vector.tensor_tensor(m1, k4, cosL.unsqueeze(2).to_broadcast([P, NT, 2, 16]), ALU.mult)
            nc.vector.tensor_tensor(m2[:, :, 0, :], k4[:, :, 1, :], sinL[:, :, 0:16], ALU.mult)
            step(nc.vector.tensor_tensor(m2[:, :, 1, :], k4[:, :, 0, :], sinL[:, :, 16:32], ALU.mult))
            nc.vector.tensor_tensor(pairs(krr[:, :, :], 16), m1, m2, ALU.add).then_inc(krr_ready, 1)
            dve.wait_ge(krr_ready, 1)

            def rotate(n):
                t, group = n % NT, 1 + n // NT
                r = stat[:, 0, t, 3:4]
                dve.wait_ge(proj, NT * group + t + 1)
                if n >= 2:
                    dve.wait_ge(roped, n - 1)
                src = ps[4 + t][:, :].rearrange("p (h s d) -> p h s d", h=HEADS, s=2)
                o1 = rt1[:, n % 2, :].rearrange("p (g d) -> p g d", d=32)
                o2 = rt2[:, n % 2, :].rearrange("p (h s d) -> p h s d", h=HEADS, s=2)

                def product(o, i, table, g):
                    return nc.vector.scalar_tensor_tensor(out=o, in0=i, scalar=r, op0=ALU.mult, op1=ALU.mult,
                                                          in1=table.unsqueeze(1).to_broadcast([P, g, 32]))

                product(o1, ps[4 + t][:, :].rearrange("p (g d) -> p g d", d=32), cosM[:, t, :], 2 * HEADS)
                for s in range(2):
                    last = product(o2[:, :, s, :], src[:, :, 1 - s, :], sinM[:, t, 32 * s:32 * s + 32], HEADS)
                last.then_inc(rope_m, 1)

            in_lo(4)
            for t in range(NT):
                rotate(t)
            for j in range(3):
                dve.wait_ge(ch, j + 1)
                lo_part(cT_lo[:, j, :], ps[j][:, :], cT_hi[:, j, :]).then_inc(cl, 1)
            dve.wait_ge(krh, 2)
            for i in range(2):
                lo_part(kT_lo[i][NOPE:QH, :], ps[3][0:ROPE, :], kT_hi[i][NOPE:QH, :]).then_inc(krl, 1)
            in_lo(5)
            dve.wait_ge(wh_ready, Q_CH + 1)
            w = slice(0, 2 * HEADS * QH)
            lo_part(w_lo[Q_CH % 2][:, w], raw[Q_CH % 2][:, w], w_hi[Q_CH % 2][:, w]).then_inc(w_ready, 1)
            dve.wait_ge(wh_ready, KV_CH + 1)
            lo_part(wkv_lo[:, :], raw[KV_CH % 2][:, 0:HEADS * P], wkv_hi[:, :]).then_inc(w_ready, 1)
            for t in range(NT):
                rotate(NT + t)
            dve.wait_ge(roped, 2 * NT)
            for t in range(NT):
                dve.wait_ge(qup_c, 2 * t + 2)
                q4 = q_nat[:, t, :].rearrange("p (h c) -> p h c", c=QH)[:, :, NOPE:QH].rearrange("p h (s d) -> p h s d", s=2)
                m1 = rt1[:, t % 2, 0:HEADS * ROPE].rearrange("p (h s d) -> p h s d", h=HEADS, s=2)
                m2 = rt2[:, t % 2, 0:HEADS * ROPE].rearrange("p (h s d) -> p h s d", h=HEADS, s=2)
                cs = cosL[:, t, :].unsqueeze(1).unsqueeze(1).to_broadcast([P, HEADS, 2, 16])
                nc.vector.tensor_tensor(m1, q4, cs, ALU.mult)
                for s in range(2):
                    last = nc.vector.tensor_tensor(m2[:, :, s, :], q4[:, :, 1 - s, :],
                                                   sinL[:, t, 16 * s:16 * s + 16].unsqueeze(1).to_broadcast([P, HEADS, 16]),
                                                   ALU.mult)
                step(last)
                nc.vector.tensor_tensor(q4, m1, m2, ALU.add).then_inc(q_roped, 1)
                if t == 1:
                    in_lo(6)
            for t in range(NT):
                dve.wait_ge(vh, t + 1)
                lo_part(v_lo[:, 0, t, :], ps[t][:, :], v_hi[:, 0, t, :]).then_inc(vl, 1)
            in_lo(7)

            def maxes(i):
                for n, t in enumerate(S_ORDER):
                    b, c = S_AT[t]
                    dve.wait_ge(s_full, 3 * i + min(n + 1, 3))
                    last = nc.vector.reduce_max(mx[:, i % 2, t:t + 1], ps[b][:, c:c + P * (t + 1)], AX_X)
                    if n in (0, 3):
                        step(last)
                        w = slice(t, t + 1) if n == 0 else slice(0, 3)
                        nc.vector.tensor_scalar(nb[:, i % 2, w], mx[:, i % 2, w], -SCALE[i], None,
                                                ALU.mult).then_inc(s_nb, 1)

            def inverse_sums(i, n):
                dve.wait_ge(s_exp, NT * i + (1, NT)[n])
                if i >= 2:
                    dve.wait_ge(s_norm, NT * (i - 1))
                w = (slice(3, 4), slice(0, 3))[n]
                nc.vector.reciprocal(ri[:, i % 2, w], rs[:, i % 2, w]).then_inc(s_ri, 1)

            def q_part(i):
                if prepared(i):
                    dve.wait_ge(qh, preps(i))
                    rows = QH if i < HEADS else P
                    s = slot(i)
                    lo_part(qT_lo[s][0:rows, :], ps[qk_banks(i)[0]][0:rows, :], qT_hi[s][0:rows, :]).then_inc(ql, 1)

            def k_part(i):
                if prepared(i):
                    dve.wait_ge(kh, preps(i))
                    rows = NOPE if i < HEADS else P
                    s = slot(i)
                    lo_part(kT_lo[s][0:rows, :], ps[qk_banks(i)[1]][0:rows, :], kT_hi[s][0:rows, :]).then_inc(kl, 1)

            def p_part(i):
                for n, (b, c, w) in enumerate(PT_COPY):
                    dve.wait_ge(ph, 3 * i + n + 1)
                    lo_part(pT_lo[:, c:c + w], ps[b][:, 0:w], pT_hi[:, c:c + w]).then_inc(pl, 1)

            def o_part(i):
                dve.wait_ge(oh, i + 1)
                r0 = VD * (i % 2)
                lo_part(uT_lo[r0:r0 + VD, i // 2, :], ps[6][0:VD, :], uT_hi[r0:r0 + VD, i // 2, :]).then_inc(ol, 1)

            for i in (0, 1):
                q_part(i)
                k_part(i)
            maxes(0)
            inverse_sums(0, 0)
            inverse_sums(0, 1)
            for t in range(NT):
                dve.wait_ge(vh, NT + t + 1)
                lo_scaled(v_lo[:, 1, t, :], ps[4 + t][:, :], stat[:, 0, t, 3:4], v_hi[:, 1, t, :]).then_inc(vl, 1)
            q_part(2)
            k_part(2)
            for i in range(NH + 1):
                if i >= 1:
                    p_part(i - 1)
                if i + 1 < NH:
                    maxes(i + 1)
                q_part(i + 3)
                if i + 1 < NH:
                    inverse_sums(i + 1, 0)
                    inverse_sums(i + 1, 1)
                if i >= 1:
                    o_part(i - 1)
                k_part(i + 3)

            def mlp_lo(j, r, gains=True):
                dve.wait_ge(wh_ready, r + (1 - NO))
                if gains:
                    for k in range(ND):
                        w = slice(256 * k, 256 * k + 256)
                        last = lo_scaled(w_lo[j][:, w], raw[j][:, w], g_up[:, k:k + 1], w_hi[j][:, w])
                else:
                    last = lo_part(w_lo[j][:, :], raw[j][:, :], w_hi[j][:, :])
                last.then_inc(w_ready, 1)

            for j in range(2):
                mlp_lo(j, UP_CH + j)

            halves = [0]

            def scaled(norm, t, n_rstd, n_g):
                dve.wait_ge(g_post_in, n_g)
                dve.wait_ge(rstd, n_rstd)
                for b in range(2):
                    w = slice(TOP * b, TOP * b + TOP)
                    if halves[0] >= 2:
                        dve.wait_ge(h_ready, halves[0] - 1)
                    halves[0] += 1
                    nc.vector.scalar_tensor_tensor(out=un[:, w], in0=ps[2 * t + b][:, :], scalar=stat[:, norm, t, 3:4],
                                                   in1=post_g[:, w], op0=ALU.mult, op1=ALU.mult).then_inc(y_s, 1)
                    dve.wait_ge(y_s, halves[0])
                    nc.vector.tensor_tensor(h_sb[:, t, w], h_sb[:, t, w], un[:, w], ALU.add).then_inc(h_ready, 1)

            for t in range(NT):
                dve.wait_ge(h_in[t], 16)
                scaled(3, t, 3 * NT + t + 1, 16)
                if t >= 1:
                    transposed_lo(2 * NT, t - 1)
            transposed_lo(2 * NT, NT - 1)

            def up_step(i, first=False, last=False):
                for j in range(2):
                    if not (first and j == 0):
                        mlp_lo(1 - j, i * 2 + (UP_CH + j + 1), not (last and j == 1))
                    for m in range(2):
                        dve.wait_ge(relu_c, i * 4 + (2 * j + m + 1))
                        nc.vector.tensor_tensor(act_sb[:, bass.ds(i * 4 + (2 * j + m), 1), :], relu[:, m:m + 1, :],
                                                relu[:, m:m + 1, :], ALU.mult).then_inc(a_ready, 1)

            def down_a(j, c):
                dve.wait_ge(ah, c + 1)
                lo_part(a_lo[j][:, :, :], act_sb[:, bass.ds(c * 2, 2), :], a_hi[j][:, :, :]).then_inc(al, 1)

            up_step(0, first=True)
            down_a(0, 0)
            with dve.Fori(1, NF // 4 - 1) as i:
                up_step(i)
            up_step(NF // 4 - 1, last=True)

            def down_lo(j, c):
                mlp_lo(j, c + DOWN_CH, False)
                down_a(j, c)

            down_lo(1, 1)
            with dve.Fori(1, NF // 4) as i:
                for j in range(2):
                    down_lo(j, i * 2 + j)
            for t in range(NT):
                scaled(5, t, 5 * NT + t + 1, 32)

        @block.tensor
        def _(pe):
            def mm3(out, lh, ll, rh, rl, start, stop):
                nc.tensor.matmul(out, lh, rh, start=start, stop=False)
                nc.tensor.matmul(out, lh, rl, start=False, stop=False)
                return nc.tensor.matmul(out, ll, rh, start=False, stop=stop)

            def transposes(src, t):
                for k in range(ND):
                    last = nc.tensor.transpose(ps[2 * t + k // 4][:, P * (k % 4):P * (k % 4) + P],
                                               src[:, t, P * k:P * k + P], ident[:, :])
                    if k % 4 == 3:
                        last.then_inc(uT_full, 1)

            def group(g, before_tile):
                n = GROUP_COLS[g][1]
                for part in range(2):
                    r = IN_CH[2 * g + part]
                    for t in range(NT):
                        before_tile(part, t)
                        if t == 0:
                            pe.wait_ge(w_ready, r + 1)
                        tok = slice(P * t, P * t + P)
                        for k in range(4):
                            w = slice(n * k, n * k + n)
                            last = mm3(ps[4 * (g > 0) + t][:, 0:n], uT_hi[:, 4 * part + k, tok], uT_lo[:, 4 * part + k, tok],
                                       w_hi[r % 2][:, w], w_lo[r % 2][:, w], part == 0 and k == 0, part == 1 and k == 3)
                        if part == 1:
                            last.then_inc(proj, 1)
                    if part == 0:
                        last.then_inc(w_used, 1)

            def input_tile(t):
                pe.wait_ge(x_in[t], 16)
                transposes(x_sb, t)

            def before_latents(part, t):
                if part == 0:
                    if t == 0:
                        input_tile(0)
                    if t + 1 < NT:
                        input_tile(t + 1)
                    pe.wait_ge(ul, 2 * t + 2)

            pe.wait_ge(consts, 3)
            group(0, before_latents)
            group(1, lambda part, t: None)
            pe.wait_ge(cn_ready, 2 * NT)
            for j in range(3):
                for t in range(NT):
                    last = nc.tensor.transpose(ps[j][:, P * t:P * t + P], cn[:, t, P * j:P * j + P], ident[:, :])
                last.then_inc(cT_full, 1)
            pe.wait_ge(krr_ready, 1)
            for t in range(NT):
                last = nc.tensor.transpose(ps[3][0:ROPE, P * t:P * t + P], krr[:, t, :], ident[:, :])
            last.then_inc(krT_full, 1)
            group(2, lambda part, t: part == 0 and pe.wait_ge(rope_m, t + 1))
            pe.wait_ge(w_ready, Q_CH + 1)
            pe.wait_ge(cl, 3)
            pe.wait_ge(krl, 2)
            for n in range(2 * NT):
                t, hf = n // 2, n % 2
                if n >= NT:
                    pe.wait_ge(rope_m, n + 1)
                for k in range(2):
                    w = slice(HEADS * QH * k + 4 * QH * hf, HEADS * QH * k + 4 * QH * (hf + 1))
                    last = mm3(ps[n][:, 0:4 * QH], cT_hi[:, k, P * t:P * t + P], cT_lo[:, k, P * t:P * t + P],
                               w_hi[Q_CH % 2][:, w], w_lo[Q_CH % 2][:, w], k == 0, k == 1)
                last.then_inc(qup, 1)
            pe.wait_ge(w_ready, KV_CH + 1)
            wv_hi = wkv_hi[:, :].rearrange("p (h c) -> p h c", c=P)[:, :, NOPE:]
            wv_lo = wkv_lo[:, :].rearrange("p (h c) -> p h c", c=P)[:, :, NOPE:]
            for t in range(NT):
                pe.wait_ge(qup_c, t + 1)
                last = mm3(ps[t][:, :].rearrange("p (h c) -> p h c", c=VD), cT_hi[:, 2, P * t:P * t + P],
                           cT_lo[:, 2, P * t:P * t + P], wv_hi, wv_lo, True, True)
                last.then_inc(v_full, 1)

            def q_prep(i):
                if prepared(i):
                    if i == 0:
                        pe.wait_ge(vl, NT)
                        pe.wait_ge(q_roped, NT)
                    elif i == 3:
                        pe.wait_ge(ql, preps(i) - 1)
                    elif i > 3:
                        pe.wait_ge(pl, 3 * (i - 4) + 1)
                    if i == HEADS:
                        pe.wait_ge(roped, 2 * NT)
                    b, rows = qk_banks(i)[0], QH if i < HEADS else P
                    src, c0 = (q_nat, QH * i) if i < HEADS else (mq_nat, MOBA_D * (i - HEADS))
                    for t in range(NT):
                        last = nc.tensor.transpose(ps[b][0:rows, P * t:P * t + P], src[:, t, c0:c0 + rows], ident[:, :])
                    last.then_inc(qT_full, 1)

            def k_prep(i):
                if prepared(i):
                    b = qk_banks(i)[1]
                    if i == 2:
                        pe.wait_ge(vl, 2 * NT)
                    elif i > 2:
                        pe.wait_ge(kl, preps(i) - 1)
                    if i < HEADS:
                        w = slice(P * i, P * i + P)
                        last = mm3(ps[b][:, :], wkv_hi[:, w], wkv_lo[:, w], cT_hi[:, 2, :], cT_lo[:, 2, :], True, True)
                    else:
                        c0 = MOBA_D * (i - HEADS)
                        for t in range(NT):
                            last = nc.tensor.transpose(ps[b][:, P * t:P * t + P], mk_nat[:, t, c0:c0 + P], ident[:, :])
                    last.then_inc(kT_full, 1)

            def scores(i):
                pe.wait_ge(kl, 2 if i == 0 else preps(i))
                s, r = slot(i), slice(0, QH)
                if i >= HEADS:
                    r = slice(MOBA_D * (i % 2), MOBA_D * (i % 2) + MOBA_D)
                for n, t in enumerate(S_ORDER):
                    b, c = S_AT[t]
                    if i >= 1:
                        pe.wait_ge(s_exp, NT * (i - 1) + (n + 1 if n < 2 else NT))
                    w, tok = P * (t + 1), slice(P * t, P * t + P)
                    mm3(ps[b][:, c:c + w], qT_hi[s][r, tok], qT_lo[s][r, tok], kT_hi[s][r, 0:w], kT_lo[s][r, 0:w],
                        True, False)
                    last = nc.tensor.matmul(ps[b][:, c + w - P:c + w], ident_b[:, :], mask_b[:, :], start=False, stop=True)
                    if n != 2:
                        last.then_inc(s_full, 1)

            def before_values(part, t):
                if part == 0:
                    pe.wait_ge(qup_c, NT + t + 1)
                elif t == 0:
                    for i in (0, 1):
                        q_prep(i)
                        k_prep(i)
                elif t == 2:
                    scores(0)

            group(3, before_values)

            def probs_T(i):
                pe.wait_ge(s_norm, NT * (i + 1))
                for k in PT_ORDER:
                    b, c = PT_AT[k]
                    if k == 0:
                        j = max(j for j in range(min(i + 4, NH)) if prepared(j))
                        pe.wait_ge(ql, preps(j))
                    if i >= 1 and k in (1, 2):
                        pe.wait_ge(pl, 3 * (i - 1) + k + 1)
                    for t in range(k, NT):
                        last = nc.tensor.transpose(ps[b][:, c + P * (t - k):c + P * (t - k) + P],
                                                   probs[i % 2][:, p_off(t) + P * k:p_off(t) + P * k + P], ident[:, :])
                    if k != 1:
                        last.then_inc(pT_full, 1)

            def weighted(i):
                pe.wait_ge(pl, 3 * (i + 1))
                if i >= 1:
                    pe.wait_ge(ol, i)
                g, vc = i // HEADS, slice(VD * (i % HEADS), VD * (i % HEADS) + VD)
                for k in range(NT):
                    w = slice(PT_OFF[k], PT_OFF[k] + P * (NT - k))
                    out_k, stop = ps[6][:, P * k:TOP], k == NT - 1
                    last = mm3(out_k[0:VD], v_hi[:, g, k, vc], v_lo[:, g, k, vc], pT_hi[:, w], pT_lo[:, w], k == 0, stop)
                last.then_inc(o_full, 1)

            q_prep(2)
            k_prep(2)
            for i in range(NH + 1):
                if i >= 1:
                    probs_T(i - 1)
                if i + 1 < NH:
                    scores(i + 1)
                q_prep(i + 3)
                if i >= 1:
                    weighted(i - 1)
                k_prep(i + 3)

            def out_rows(t, b, c, kk):
                tok, k = slice(P * t, P * t + P), 2 * c + kk
                hi, lo = (w_hi[c], w_lo[c]) if c < 2 else (wo_hi[c - 2], wo_lo[c - 2])
                w = slice(D * kk + TOP * b, D * kk + TOP * b + TOP)
                return mm3(ps[2 * t + b][:, :], uT_hi[:, k, tok], uT_lo[:, k, tok], hi[:, w], lo[:, w], k == 0, k == ND - 1)

            for c in range(2):
                pe.wait_ge(wo_ready, c + 1)
                for t in range(NT):
                    if c == 0 and t == NT - 1:
                        pe.wait_ge(ol, NH)
                    for kk in range(2):
                        for b in range(2):
                            last = out_rows(t, b, c, kk)
                last.then_inc(w_used, 1)
            pe.wait_ge(wo_ready, NO)
            for t in range(NT):
                for b in range(2):
                    for c in (2, 3):
                        for kk in range(2):
                            last = out_rows(t, b, c, kk)
                    last.then_inc(y_full, 1)
                if t >= 1:
                    pe.wait_ge(h_ready, 2 * t)
                    transposes(h_sb, t - 1)

            def up_block(bank, j, m, tok):
                for k in range(ND):
                    w = slice(256 * k + P * m, 256 * k + P * m + P)
                    last = mm3(ps[bank][:, tok], w_hi[j][:, w], w_lo[j][:, w], uT_hi[:, k, tok], uT_lo[:, k, tok],
                               k == 0, k == ND - 1)
                return last

            A, B = slice(0, 2 * P), slice(2 * P, 4 * P)
            pe.wait_ge(w_ready, UP_CH + 2 - NO)
            pe.wait_ge(ul, 2 * NT + 4)
            up_block(0, 0, 0, A)
            up_block(1, 0, 1, A)
            pe.wait_ge(h_ready, 2 * NT)
            transposes(h_sb, NT - 1)
            up_block(2, 1, 0, A)
            pe.wait_ge(ul, 4 * NT)
            for bank in range(3):
                up_block(bank, bank // 2, bank % 2, B).then_inc(up_full, 1)
            up_block(3, 1, 1, slice(0, S)).then_inc(up_full, 1)
            with pe.Fori(1, NF // 4) as i:
                for j in range(2):
                    pe.wait_ge(w_ready, i * 2 + (UP_CH + j + 1 - NO))
                    for m in range(2):
                        pe.wait_ge(relu_c, i * 4 + (2 * j + m - 3))
                        up_block(2 * j + m, j, m, slice(0, S)).then_inc(up_full, 1)

            def down_rows(t, b, j, kk, start, stop):
                tok = slice(P * t, P * t + P)
                w = slice(D * kk + TOP * b, D * kk + TOP * b + TOP)
                return mm3(ps[2 * t + b][:, :], a_hi[j][:, kk, tok], a_lo[j][:, kk, tok], w_hi[j][:, w], w_lo[j][:, w],
                           start, stop)

            def down_chunk(j, c, first=False):
                pe.wait_ge(w_ready, c + (DOWN_CH + 1 - NO))
                pe.wait_ge(al, c + 1)
                for t in ((2, 3, 0, 1) if first else range(NT)):
                    if first and t < 2:
                        pe.wait_ge(relu_c, NF - 2 * (1 - t))
                    for kk in range(2):
                        for b in range(2):
                            last = down_rows(t, b, j, kk, first and kk == 0, False)
                last.then_inc(w_used, 1)

            down_chunk(0, 0, True)
            down_chunk(1, 1)
            with pe.Fori(1, NF // 4 - 1) as i:
                down_chunk(0, i * 2)
                down_chunk(1, i * 2 + 1)
            def last_rows(t, j, b):
                for kk in range(2):
                    last = down_rows(t, b, j, kk, False, j == 1 and kk == 1)
                return last

            pe.wait_ge(w_ready, DOWN_CH - NO + NF // 2 - 1)
            pe.wait_ge(al, NF // 2 - 1)
            for t in (0, 1):
                for b in range(2):
                    last_rows(t, 0, b)
            pe.wait_ge(w_ready, DOWN_CH - NO + NF // 2)
            pe.wait_ge(al, NF // 2)
            for t in range(NT):
                for b in range(2):
                    if t >= 2:
                        last_rows(t, 0, b)
                    last_rows(t, 1, b).then_inc(y_full, 1)


def rope_constants(seq):
    import numpy as np

    cols = []
    for half in (MOBA_D // 2, ROPE // 2):
        inv = (np.float32(1.0) / np.float32(10000.0) ** (np.arange(half, dtype=np.float32) / np.float32(half))).astype(np.float32)
        ang = (np.arange(seq, dtype=np.float32)[:, None] * inv[None, :]).astype(np.float32)
        c, s = np.cos(ang).astype(np.float32), np.sin(ang).astype(np.float32)
        cols += [c, -s, s]
    return np.ascontiguousarray(np.concatenate(cols, axis=1))


NAMES = ["x", "attn_pre_g", "w_in", "mla_q_norm_g", "w_mla_q_up", "mla_kv_norm_g", "w_mla_kv_up", "w_out",
         "attn_post_g", "mlp_pre_g", "w_up", "w_down", "mlp_post_g"]


def kernel(**inputs):
    import numpy as np
    import concourse.bacc as bacc
    from concourse.bass_utils import run_bass_kernel_spmd

    nc = bacc.Bacc("TRN2", target_bir_lowering=False, num_devices=1)
    arrays = {name: np.ascontiguousarray(inputs[name]) for name in NAMES}
    arrays["rope_table"] = rope_constants(arrays["x"].shape[1])
    args = [nc.dram_tensor(f"in_{name}", a.shape, mybir.dt.from_np(a.dtype), kind="ExternalInput").ap()
            for name, a in arrays.items()]
    out = nc.dram_tensor("out", arrays["x"].shape, F32, kind="ExternalOutput").ap()
    build(nc, *args, out)
    r = run_bass_kernel_spmd(nc, [{f"in_{name}": a for name, a in arrays.items()}], core_ids=[0])
    return r.results[0]["out"]
```

```python
from contextlib import ExitStack

import concourse.bass as bass
from concourse import mybir

F32 = mybir.dt.float32
F32R = mybir.dt.float32r
BF16 = mybir.dt.bfloat16
ALU = mybir.AluOpType
ACT = mybir.ActivationFunctionType
AX_X = mybir.AxisListType.X

P = 128
EPS = 1e-6
NEG = -1e30
NOPE, ROPE, VD = 64, 32, 64
HEADS = 8
MOBA_D = 64
TOP = 512


def build(nc, x, attn_pre_g, w_in, mla_q_norm_g, w_mla_q_up, mla_kv_norm_g, w_mla_kv_up, w_out,
          attn_post_g, mlp_pre_g, w_up, w_down, mlp_post_g, rope_table, out):
    S, D = x.shape[1], x.shape[2]
    F = w_up.shape[2]
    QR, KVR = w_mla_q_up.shape[1], w_mla_kv_up.shape[1]
    NT = S // P
    ND = D // P
    NF = F // P
    CA = QR + KVR + ROPE
    HW = HEADS * MOBA_D
    QH = NOPE + ROPE
    CW = 2048
    NH = 2 * HEADS
    SCALE = [float(QH) ** -0.5] * HEADS + [float(MOBA_D) ** -0.5] * HEADS
    assert (S, D, F, NT, CA) == (512, 1024, 4096, 4, 416)

    x_v = x[0].rearrange("(t p) d -> t p d", p=P)
    out_v = out[0].rearrange("(t p) d -> t p d", p=P)
    w_in_v = w_in[0].rearrange("(k p) n -> p k n", p=P)
    w_q_v = w_mla_q_up[0].rearrange("(k p) n -> p k n", p=P)
    w_out_v = w_out[0].rearrange("(k p) n -> p k n", p=P)
    w_up_v = w_up[0].rearrange("(k p) n -> p k n", p=P)
    w_down_v = w_down[0].rearrange("(k p) n -> p k n", p=P)

    IN_CH = [0, 1, 2, 3, 4, 5, 8, 9]
    Q_CH, KV_CH = 6, 7
    OUT_CH = [10, 11, 12, 13]
    UP_CH = 14
    DOWN_CH = UP_CH + NF // 2
    NO = len(OUT_CH)

    def w_slot(r):
        return 1 - r % 2 if r > KV_CH else r % 2

    GROUP_COLS = [(0, CA), (CA, HW), (CA + HW, HW), (CA + 2 * HW, HW)]
    TRI = NT * (NT + 1) // 2 * P

    with ExitStack() as ctx:
        def sb(name, shape, dt=F32, stack=ctx):
            return stack.enter_context(nc.sbuf_tensor(name, shape, dt))

        def sem(name):
            return ctx.enter_context(nc.semaphore(name))

        uT_hi = sb("uT_hi", [P, ND, S], F32R)
        uT_lo = sb("uT_lo", [P, ND, S], F32R)
        raw = [sb(f"w_raw{i}", [P, CW]) for i in range(2)]
        w_hi = [sb(f"w_hi{i}", [P, CW], F32R) for i in range(2)]
        w_lo = [sb(f"w_lo{i}", [P, CW], F32R) for i in range(2)]
        g_in = sb("g_in", [P, ND])
        g_up = sb("g_up", [P, ND])
        ident = sb("ident", [P, P])
        ident_b = sb("ident_b", [P, P], BF16)
        mask_b = sb("mask_b", [P, P], BF16)
        half = sb("half", [P, 1])
        stat = sb("stat", [P, 6, NT, 4])
        att = ExitStack()
        with ExitStack() as mla:
            cT_hi = sb("cT_hi", [P, 3, S], F32R, stack=mla)
            cT_lo = sb("cT_lo", [P, 3, S], F32R, stack=mla)
            wkv_hi = sb("wkv_hi", [P, HEADS * P], F32R, stack=mla)
            wkv_lo = sb("wkv_lo", [P, HEADS * P], F32R, stack=mla)
            q_nat = sb("q_nat", [P, NT, HEADS * QH], stack=mla)
        wo_hi = [sb(f"wo_hi{i}", [P, CW], F32R, stack=att) for i in range(2)]
        wo_lo = [sb(f"wo_lo{i}", [P, CW], F32R, stack=att) for i in range(2)]
        mq_nat = sb("mq_nat", [P, NT, HW], stack=att)
        mk_nat = sb("mk_nat", [P, NT, HW], stack=att)
        with ExitStack() as start:
            x_sb = sb("x_sb", [P, NT, D], stack=start)
            junk_pre = sb("junk_pre", [P, D], BF16, stack=start)
        v_hi = sb("v_hi", [P, 2, NT, HW], F32R, stack=att)
        v_lo = sb("v_lo", [P, 2, NT, HW], F32R, stack=att)
        qT_hi = [sb(f"qT_hi{i}", [P, S], F32R, stack=att) for i in range(2)]
        qT_lo = [sb(f"qT_lo{i}", [P, S], F32R, stack=att) for i in range(2)]
        kT_hi = [sb(f"kT_hi{i}", [P, S], F32R, stack=att) for i in range(2)]
        kT_lo = [sb(f"kT_lo{i}", [P, S], F32R, stack=att) for i in range(2)]
        mx = sb("mx", [P, 2, NT], stack=att)
        nb = sb("nb", [P, 2, NT], stack=att)
        rs = sb("rs", [P, 2, NT], stack=att)
        ri = sb("ri", [P, 2, NT], stack=att)
        with ExitStack() as pre:
            lat_g = sb("lat_g", [P, QR + KVR], stack=pre)
            rope_sb = sb("rope_sb", [P, NT, rope_table.shape[1]], stack=pre)
            cn = sb("cn", [P, NT, QR + KVR], stack=pre)
            kr = sb("kr", [P, NT, ROPE], stack=pre)
            krr = sb("krr", [P, NT, ROPE], stack=pre)
            rt1 = sb("rt1", [P, 2, HW], stack=pre)
            rt2 = sb("rt2", [P, 2, HW], stack=pre)
        probs = [sb(f"probs{i}", [P, TRI], stack=att) for i in range(2)]
        pT_hi = [sb(f"pT_hi{i}", [P, TRI], F32R, stack=att) for i in range(2)]
        pT_lo = [sb(f"pT_lo{i}", [P, TRI], F32R, stack=att) for i in range(2)]
        att.close()
        act_sb = sb("act_sb", [P, NF, S])
        h_sb = sb("h_sb", [P, NT, D])
        relu = sb("relu", [P, 2, S])
        a_hi = [sb(f"a_hi{i}", [P, 2, S], F32R) for i in range(2)]
        a_lo = [sb(f"a_lo{i}", [P, 2, S], F32R) for i in range(2)]
        post_g = sb("post_g", [P, D])
        un = sb("un", [P, D])
        junk_post = sb("junk_post", [P, D], BF16)

        ps = [ctx.enter_context(nc.psum_tensor(f"bank{b}", [P, TOP], F32)) for b in range(8)]

        x_in = [[sem(f"x{t}{b}_in") for b in "lr"] for t in range(NT)]
        h_in = [sem(f"h{t}_in") for t in range(NT)]
        g_in_in, g_up_in, g_post_in = sem("g_in_in"), sem("g_up_in"), sem("g_post_in")
        tab_in, lat_in = sem("tab_in"), sem("lat_in")
        raw_in = [sem(f"raw{i}_in") for i in range(2)]
        first_in = sem("first_in")
        first_h, first_ready = sem("first_h"), sem("first_ready")
        wh_ready = sem("wh_ready")
        w_ready = sem("w_ready")
        wo_hi_ready = sem("wo_hi_ready")
        wo_ready = sem("wo_ready")
        w_used = sem("w_used")
        zeroed, consts = sem("zeroed"), sem("consts")
        sq = sem("sq")
        pool_step = sem("pool_step")
        dve_step = sem("dve_step")
        rstd = sem("rstd")
        uT_full = sem("uT_full")
        uh = sem("uh")
        ul = sem("ul")
        proj = sem("proj")
        kr_c, krr_ready = sem("kr_c"), sem("krr_ready")
        cn_ready = sem("cn_ready")
        rope_m = sem("rope_m")
        roped = sem("roped")
        cT_full, krT_full = sem("cT_full"), sem("krT_full")
        ch, cl = sem("ch"), sem("cl")
        krh, krl = sem("krh"), sem("krl")
        qup, qup_c, q_roped = sem("qup"), sem("qup_c"), sem("q_roped")
        v_full, vh, vl = sem("v_full"), sem("vh"), sem("vl")
        qT_full, qh, ql = sem("qT_full"), sem("qh"), sem("ql")
        kT_full, kh, kl = sem("kT_full"), sem("kh"), sem("kl")
        s_full, s_nb, s_exp = sem("s_full"), sem("s_nb"), sem("s_exp")
        s_ri, s_norm = sem("s_ri"), sem("s_norm")
        pT_full, ph, pl = sem("pT_full"), sem("ph"), sem("pl")
        o_full, oh, ol = sem("o_full"), sem("oh"), sem("ol")
        y_full = sem("y_full")
        y_s = sem("y_s")
        h_ready = sem("h_ready")
        up_full, relu_c, a_ready = sem("up_full"), sem("relu_c"), sem("a_ready")
        ah, al = sem("ah"), sem("al")
        out_done = sem("out_done")

        def p_off(t):
            return P * (t * (t + 1) // 2)

        PT_OFF = [0, TOP, 2 * TOP, 2 * TOP - P]

        def slot(i):
            return i % 2 if i < HEADS else (i // 2) % 2

        def before(i):
            return i - 2 if i <= HEADS else i - 3

        def prepared(i):
            return i < NH and (i < HEADS or i % 2 == 0)

        def preps(i):
            return i + 1 if i < HEADS else HEADS + (i - HEADS) // 2 + 1

        def qk_banks(i):
            return [(0, 1), (2, 3), (3, 6)][i] if i < 3 else (3, 7)

        S_AT = [(0, 0), (1, 0), (0, P), (2, 0)]
        S_ORDER = [3, 1, 0, 2]
        PT_AT = [(3, 0), (4, 0), (5, 0), (4, 3 * P)]
        PT_ORDER = [0, 1, 3, 2]
        PT_COPY = [(3, 0, TOP), (4, TOP, TOP), (5, 2 * TOP, 2 * P)]
        PIECE = 512
        OUT_PIECES = {i: [i - 4] if i < HEADS else [2 * i - 12, 2 * i - 11] for i in range(4, 14)}

        block = ctx.enter_context(nc.Block())

        @block.sync
        def _(sp):
            def chunk(r, src, n):
                if r - 2 in OUT_CH:
                    sp.wait_ge(wo_ready, OUT_CH.index(r - 2) + 1)
                elif r >= 2:
                    sp.wait_ge(w_ready, r - 1)
                k = src.shape[1]
                dst = raw[r % 2][:, 0:n].rearrange("p (k n) -> p k n", k=k)
                sp.dma_start(dst, src).then_inc(raw_in[r % 2], 16)

            def in_chunk(i):
                g, part = i // 2, i % 2
                c0, n = GROUP_COLS[g]
                chunk(IN_CH[i], w_in_v[:, 4 * part:4 * part + 4, c0:c0 + n], 4 * n)

            def x_half(t, b):
                w = slice(TOP * b, TOP * b + TOP)
                sp.dma_start(x_sb[:, t, w], x_v[t][:, w]).then_inc(x_in[t][b], 16)

            x_half(0, 0)
            for i, n in ((0, first_in), (1, raw_in[0])):
                sp.dma_start(raw[0][:, 2 * CA * i:2 * CA * (i + 1)].rearrange("p (k n) -> p k n", k=2),
                             w_in_v[:, 2 * i:2 * i + 2, 0:CA]).then_inc(n, 16)
            for t in range(1, NT):
                x_half(t, 0)
            x_half(0, 1)
            in_chunk(1)
            for t in range(1, NT):
                x_half(t, 1)
            sp.dma_start(rope_sb[:, :, :], rope_table.rearrange("(t p) c -> p t c", p=P)).then_inc(tab_in, 16)
            sp.dma_start(lat_g[:, 0:QR], mla_q_norm_g.to_broadcast([P, QR])).then_inc(lat_in, 16)
            sp.dma_start(lat_g[:, QR:], mla_kv_norm_g.to_broadcast([P, KVR])).then_inc(lat_in, 16)
            for i in range(2, 6):
                in_chunk(i)
            sp.dma_start(g_up[:, :], mlp_pre_g[0].rearrange("(k p) -> p k", p=P), allow_slow_non_contiguous=True).then_inc(g_up_in, 16)
            chunk(Q_CH, w_q_v, 2 * HEADS * QH)
            chunk(KV_CH, w_mla_kv_up.rearrange("o p n -> p o n"), HEADS * P)
            in_chunk(6)
            in_chunk(7)
            for i, r in enumerate(OUT_CH):
                chunk(r, w_out_v[:, 2 * i:2 * i + 2, :], CW)
            sp.wait_ge(o_full, NH)
            for t in range(NT):
                sp.dma_start(h_sb[:, t, :], x_v[t]).then_inc(h_in[t], 16)
            sp.dma_start(post_g[:, :], attn_post_g.to_broadcast([P, D])).then_inc(g_post_in, 16)
            for j in range(2):
                chunk(UP_CH + j, w_up_v[:, :, 256 * j:256 * j + 256], CW)
            with sp.Fori(1, NF // 4) as i:
                for j in range(2):
                    sp.wait_ge(w_ready, i * 2 + (UP_CH + j - 1 - NO))
                    sp.dma_start(raw[j][:, :].rearrange("p (k n) -> p k n", k=ND),
                                 w_up_v[:, :, bass.ds(i * 512 + j * 256, 256)]).then_inc(raw_in[j], 16)
            with sp.Fori(0, NF // 4) as i:
                for j in range(2):
                    sp.wait_ge(w_ready, i * 2 + (DOWN_CH + j - 1 - NO))
                    sp.dma_start(raw[j][:, :].rearrange("p (k n) -> p k n", k=2),
                                 w_down_v[:, bass.ds(i * 4 + 2 * j, 2), :]).then_inc(raw_in[j], 16)
            sp.wait_ge(y_s, 2 * NT)
            sp.dma_start(post_g[:, :], mlp_post_g.to_broadcast([P, D])).then_inc(g_post_in, 16)
            for n in range(2 * NT):
                t, c = n // 2, TOP * (n % 2)
                sp.wait_ge(h_ready, 2 * NT + n + 1)
                sp.dma_start(out_v[t][:, c:c + TOP], h_sb[:, t, c:c + TOP]).then_inc(out_done, 16)
            sp.wait_ge(out_done, 16 * 2 * NT)

        @block.gpsimd
        def _(pool):
            nc.gpsimd.memset(ident[:, :], 0.0).then_inc(zeroed, 1)
            nc.gpsimd.memset(ident_b[:, :], 0.0).then_inc(zeroed, 1)
            nc.gpsimd.memset(mask_b[:, :], 0.0).then_inc(zeroed, 1)
            nc.gpsimd.memset(half[:, :], -0.5).then_inc(zeroed, 1)
            pool.wait_ge(zeroed, 4)
            for m in (ident, ident_b):
                nc.gpsimd.affine_select(out=m[:, :], in_=m[:, :], compare_op=ALU.not_equal, fill=1.0, base=0,
                                        pattern=[[-1, P]], channel_multiplier=1).then_inc(consts, 1)
            nc.gpsimd.affine_select(out=mask_b[:, :], in_=mask_b[:, :], compare_op=ALU.is_ge, fill=NEG, base=0,
                                    pattern=[[-1, P]], channel_multiplier=1).then_inc(consts, 1)
            own = [0]

            def step(ins):
                own[0] += 1
                ins.then_inc(pool_step, 1)
                pool.wait_ge(pool_step, own[0])

            def rms(norm, t, n, n_sq, parts=1, by=None, squared=False):
                s = stat[:, norm, t, :]
                add = EPS
                if parts == 2:
                    pool.wait_ge(sq, n_sq - 1)
                    step(nc.gpsimd.tensor_scalar(s[:, 2:3], s[:, 0:1], 1.0 / n, EPS, ALU.mult, ALU.add))
                    add = s[:, 2:3]
                pool.wait_ge(sq, n_sq)
                step(nc.gpsimd.tensor_scalar(s[:, 2:3], s[:, parts - 1:parts], 1.0 / n, add, ALU.mult, ALU.add))
                last = nc.gpsimd.tensor_tensor(s[:, 3:4], s[:, 2:3], half[:, :], ALU.pow)
                if by is not None or squared:
                    step(last)
                    last = nc.gpsimd.tensor_tensor(s[:, 3:4], s[:, 3:4], s[:, 3:4] if squared else by, ALU.mult)
                last.then_inc(rstd, 1)

            for t in range(NT):
                rms(0, t, D, t + 1)
            for t in range(NT):
                rms(1, t, QR, NT + 2 * t + 1, by=stat[:, 0, t, 3:4])
                rms(2, t, KVR, NT + 2 * t + 2, by=stat[:, 0, t, 3:4])
            for n in range(2 * NT):
                t = n % NT
                pool.wait_ge(rope_m, n + 1)
                nc.gpsimd.tensor_tensor((mq_nat, mk_nat)[n // NT][:, t, :], rt1[:, n % 2, :], rt2[:, n % 2, :],
                                        ALU.add).then_inc(roped, 1)
            def out_piece(n):
                per = CW // PIECE
                c, w = n // per, slice(PIECE * (n % per), PIECE * (n % per) + PIECE)
                s = w_slot(OUT_CH[c])
                hi, lo = (w_hi[s], w_lo[s]) if c < 2 else (wo_hi[c - 2], wo_lo[c - 2])
                pool.wait_ge(wo_hi_ready, n + 1)
                last = nc.gpsimd.tensor_tensor(lo[:, w], raw[c % 2][:, w], hi[:, w].bitcast(F32), ALU.subtract)
                if n % per == per - 1:
                    last.then_inc(wo_ready, 1)

            for i in range(NH):
                for n in OUT_PIECES.get(i - 1, []):
                    out_piece(n)
                for n, t in enumerate(S_ORDER):
                    pool.wait_ge(s_ri, 2 * i + (1 if n == 0 else 2))
                    pr = probs[i % 2][:, p_off(t):p_off(t) + P * (t + 1)]
                    nc.gpsimd.tensor_tensor(pr, pr, ri[:, i % 2, t:t + 1].to_broadcast([P, P * (t + 1)]),
                                            ALU.mult).then_inc(s_norm, 1)
            for t in range(NT):
                rms(3, t, D, 3 * NT + 2 * t + 2, parts=2)
            for t in range(NT):
                rms(4, t, D, 5 * NT + t + 1, squared=True)
            for t in range(NT):
                rms(5, t, D, 6 * NT + 2 * t + 2, parts=2)

        @block.scalar
        def _(act):
            act.dma_start(g_in[:, :], attn_pre_g[0].rearrange("(k p) -> p k", p=P), allow_slow_non_contiguous=True).then_inc(g_in_in, 16)

            SLOT_LEFT = {2: (w_used, 1), 3: (proj, NT), 4: (w_used, 2), 5: (proj, 2 * NT), 6: (w_used, 3),
                         8: (proj, 3 * NT), 9: (qup, 2 * NT), 10: (w_used, 4), 11: (proj, 4 * NT),
                         12: (kT_full, HEADS), 13: (kT_full, HEADS), 14: (w_used, 5), 15: (w_used, 6)}

            def arrived(r):
                act.wait_ge(raw_in[r % 2], 16 * (r // 2 + 1))
                if r in SLOT_LEFT:
                    act.wait_ge(*SLOT_LEFT[r])

            def hi_part(out, whole, scale=1.0):
                return nc.scalar.activation(out, whole, ACT.Copy, scale=scale)

            def in_hi(i):
                r, n = IN_CH[i], GROUP_COLS[i // 2][1]
                if i == 0:
                    act.wait_ge(first_in, 16)
                else:
                    arrived(r)
                for k in range(4):
                    if i == 0 and k >= 1:
                        last.then_inc(first_h, 1)
                        if k == 2:
                            arrived(r)
                    w, kg = slice(n * k, n * k + n), 4 * (i % 2) + k
                    last = hi_part(w_hi[w_slot(r)][:, w], raw[r % 2][:, w], g_in[:, kg:kg + 1])
                last.then_inc(wh_ready, 1)

            squares = [0]

            def square(src, norm, t, col, scale=1.0):
                if squares[0]:
                    act.wait_ge(sq, squares[0])
                squares[0] += 1
                junk = junk_pre if norm <= 2 else junk_post
                nc.scalar.activation(junk[:, 0:src.shape[1]], src, ACT.Square, scale=scale,
                                     accum_out=stat[:, norm, t, col:col + 1]).then_inc(sq, 1)

            def transposed_hi(n0, t):
                for b in range(2):
                    act.wait_ge(uT_full, n0 + 2 * t + b + 1)
                    hi_part(uT_hi[:, 4 * b:4 * b + 4, P * t:P * t + P],
                            ps[2 * t + b][:, :].rearrange("p (k n) -> p k n", k=4)).then_inc(uh, 1)

            def input_hi(t, b):
                act.wait_ge(uT_full, NT * b + t + 1)
                hi_part(uT_hi[:, 4 * b:4 * b + 4, P * t:P * t + P],
                        ps[4 + t][:, :].rearrange("p (k n) -> p k n", k=4)).then_inc(uh, 1)

            input_hi(0, 0)
            act.wait_ge(g_in_in, 16)
            in_hi(0)
            input_hi(1, 0)
            input_hi(2, 0)
            input_hi(3, 0)
            in_hi(1)
            input_hi(0, 1)
            input_hi(1, 1)
            input_hi(2, 1)
            input_hi(3, 1)
            in_hi(2)
            for t in range(NT):
                for b in range(2):
                    act.wait_ge(x_in[t][b], 16)
                square(x_sb[:, t, :], 0, t, 0)
            in_hi(3)
            for t in range(NT):
                r = stat[:, 0, t, 3:4]
                act.wait_ge(rstd, t + 1)
                act.wait_ge(proj, t + 1)
                square(ps[t][:, 0:QR], 1, t, 0, r)
                square(ps[t][:, QR:QR + KVR], 2, t, 0, r)
                hi_part(kr[:, t, :], ps[t][:, QR + KVR:CA], r).then_inc(kr_c, 1)
            in_hi(4)
            for j in range(3):
                act.wait_ge(cT_full, j + 1)
                hi_part(cT_hi[:, j, :], ps[j][:, :]).then_inc(ch, 1)
            act.wait_ge(krT_full, 1)
            for i in range(2):
                hi_part(kT_hi[i][NOPE:QH, :], ps[3][0:ROPE, :]).then_inc(krh, 1)
            in_hi(5)
            arrived(Q_CH)
            hi_part(w_hi[Q_CH % 2][:, 0:2 * HEADS * QH], raw[Q_CH % 2][:, 0:2 * HEADS * QH]).then_inc(wh_ready, 1)
            arrived(KV_CH)
            hi_part(wkv_hi[:, :], raw[KV_CH % 2][:, 0:HEADS * P]).then_inc(wh_ready, 1)
            in_hi(6)
            for n in range(2 * NT):
                act.wait_ge(qup, n + 1)
                nc.scalar.copy(q_nat[:, n // 2, 4 * QH * (n % 2):4 * QH * (n % 2 + 1)],
                               ps[n][:, 0:4 * QH]).then_inc(qup_c, 1)
            for t in range(NT):
                act.wait_ge(v_full, t + 1)
                hi_part(v_hi[:, 0, t, :], ps[t][:, :]).then_inc(vh, 1)
            in_hi(7)

            def q_part(i):
                if prepared(i):
                    act.wait_ge(qT_full, preps(i))
                    if i >= 2:
                        act.wait_ge(s_full, 3 * (before(i) + 1))
                    rows = QH if i < HEADS else P
                    hi_part(qT_hi[slot(i)][0:rows, :], ps[qk_banks(i)[0]][0:rows, :]).then_inc(qh, 1)

            def k_part(i):
                if prepared(i):
                    act.wait_ge(kT_full, preps(i))
                    if i >= 2:
                        act.wait_ge(s_full, 3 * (before(i) + 1))
                    rows = NOPE if i < HEADS else P
                    hi_part(kT_hi[slot(i)][0:rows, :], ps[qk_banks(i)[1]][0:rows, :]).then_inc(kh, 1)

            def exps(i, tiles):
                if i >= 2:
                    act.wait_ge(pT_full, 3 * (i - 1))
                for t in tiles:
                    j = S_ORDER.index(t)
                    act.wait_ge(s_nb, 2 * i + (1 if j == 0 else 2))
                    b, c = S_AT[t]
                    n = P * (t + 1)
                    nc.scalar.activation(probs[i % 2][:, p_off(t):p_off(t) + n], ps[b][:, c:c + n], ACT.Exp,
                                         bias=nb[:, i % 2, t:t + 1], scale=SCALE[i],
                                         accum_out=rs[:, i % 2, t:t + 1]).then_inc(s_exp, 1)

            def p_part(i):
                if i >= 2:
                    act.wait_ge(o_full, i - 1)
                for n, (b, c, w) in enumerate(PT_COPY):
                    act.wait_ge(pT_full, 3 * i + n + 1)
                    hi_part(pT_hi[i % 2][:, c:c + w], ps[b][:, 0:w]).then_inc(ph, 1)

            def o_part(i):
                act.wait_ge(o_full, i + 1)
                r0 = VD * (i % 2)
                hi_part(uT_hi[r0:r0 + VD, i // 2, :], ps[6][0:VD, :]).then_inc(oh, 1)

            def out_piece(n):
                per = CW // PIECE
                c, w = n // per, slice(PIECE * (n % per), PIECE * (n % per) + PIECE)
                if n % per == 0:
                    arrived(OUT_CH[c])
                hi = w_hi[w_slot(OUT_CH[c])] if c < 2 else wo_hi[c - 2]
                hi_part(hi[:, w], raw[OUT_CH[c] % 2][:, w]).then_inc(wo_hi_ready, 1)

            for i in (0, 1):
                q_part(i)
                k_part(i)
            exps(0, S_ORDER)
            for t in range(NT):
                if t == 3:
                    q_part(2)
                    exps(1, S_ORDER[:1])
                    k_part(2)
                    exps(1, S_ORDER[1:])
                act.wait_ge(proj, 3 * NT + t + 1)
                hi_part(v_hi[:, 1, t, :], ps[4 + t][:, :], stat[:, 0, t, 3:4]).then_inc(vh, 1)
            p_part(0)
            for i in range(1, NH + 2):
                if 2 <= i <= NH:
                    p_part(i - 1)
                k_part(i + 2)
                if i >= HEADS:
                    q_part(i + 2)
                for n in OUT_PIECES.get(i, []):
                    out_piece(n)
                if i + 1 < NH:
                    exps(i + 1, S_ORDER[:1])
                if i < HEADS:
                    q_part(i + 2)
                n = 1 if i >= HEADS else 3
                if i + 1 < NH:
                    exps(i + 1, S_ORDER[1:n])
                if i >= 2:
                    o_part(i - 2)
                if i + 1 < NH:
                    exps(i + 1, S_ORDER[n:])

            def mlp_hi(j, r, gains=True):
                act.wait_ge(raw_in[j], (r - j) * 8 + 16)
                if gains:
                    for k in range(ND):
                        w = slice(256 * k, 256 * k + 256)
                        last = hi_part(w_hi[1 - j][:, w], raw[j][:, w], g_up[:, k:k + 1])
                else:
                    last = hi_part(w_hi[1 - j][:, :], raw[j][:, :])
                last.then_inc(wh_ready, 1)

            act.wait_ge(g_up_in, 16)
            for j in range(2):
                act.wait_ge(*SLOT_LEFT[UP_CH + j])
                mlp_hi(j, UP_CH + j)

            def y_squares(norm, n, t, scale=1.0):
                for b in range(2):
                    act.wait_ge(y_full, 2 * n + b + 1)
                    square(ps[2 * t + b][:, :], norm, t, b, scale)

            for t in range(NT):
                y_squares(3, t, t)
                if t >= 1:
                    transposed_hi(2 * NT, t - 1)
            transposed_hi(2 * NT, NT - 1)
            for t in range(NT):
                square(h_sb[:, t, :], 4, t, 0)

            def up_step(i, first=False, last=False):
                for j in range(2):
                    if not (first and j == 0):
                        act.wait_ge(up_full, i * 4 + 2 * j)
                        mlp_hi(1 - j, i * 2 + (UP_CH + j + 1), not (last and j == 1))
                    for m in range(2):
                        act.wait_ge(up_full, i * 4 + (2 * j + m + 1))
                        if not (first and j == 0):
                            act.wait_ge(a_ready, i * 4 + (2 * j + m - 1))
                        nc.scalar.activation(relu[:, m, :], ps[2 * j + m][:, :], ACT.Relu).then_inc(relu_c, 1)

            up_step(0, first=True)
            act.wait_ge(a_ready, 2)
            hi_part(a_hi[0][:, :, :], act_sb[:, 0:2, :]).then_inc(ah, 1)
            with act.Fori(1, NF // 4 - 1) as i:
                up_step(i)
            up_step(NF // 4 - 1, last=True)

            def down_hi(j, c):
                mlp_hi(j, c + DOWN_CH, False)
                hi_part(a_hi[j][:, :, :], act_sb[:, bass.ds(c * 2, 2), :]).then_inc(ah, 1)

            act.wait_ge(up_full, NF)
            act.wait_ge(a_ready, NF)
            down_hi(1, 1)
            with act.Fori(1, NF // 4) as i:
                for j in range(2):
                    act.wait_ge(w_used, i * 2 + (j - 1 + 6))
                    down_hi(j, i * 2 + j)
            for t in range(NT):
                act.wait_ge(rstd, 4 * NT + t + 1)
                y_squares(5, NT + t, t, stat[:, 4, t, 3:4])

        @block.vector
        def _(dve):
            own = [0]

            def step(ins):
                own[0] += 1
                ins.then_inc(dve_step, 1)
                dve.wait_ge(dve_step, own[0])

            def lo_part(out, whole, hi):
                return nc.vector.tensor_tensor(out, whole, hi.bitcast(F32), ALU.subtract)

            def lo_scaled(out, whole, scale, hi):
                return nc.vector.scalar_tensor_tensor(out=out, in0=whole, scalar=scale, in1=hi.bitcast(F32),
                                                      op0=ALU.mult, op1=ALU.subtract)

            def in_lo(i):
                r, n = IN_CH[i], GROUP_COLS[i // 2][1]
                dve.wait_ge(*((first_h, 1) if i == 0 else (wh_ready, r + 1)))
                for k in range(4):
                    if i == 0 and k >= 1:
                        last.then_inc(first_ready, 1)
                        dve.wait_ge(*((first_h, k + 1) if k < 3 else (wh_ready, 1)))
                    w, kg = slice(n * k, n * k + n), 4 * (i % 2) + k
                    last = lo_scaled(w_lo[w_slot(r)][:, w], raw[r % 2][:, w], g_in[:, kg:kg + 1], w_hi[w_slot(r)][:, w])
                last.then_inc(w_ready, 1)

            def transposed_lo(n0, t):
                for b in range(2):
                    dve.wait_ge(uh, n0 + 2 * t + b + 1)
                    sl = (slice(None), slice(4 * b, 4 * b + 4), slice(P * t, P * t + P))
                    lo_part(uT_lo[sl], ps[2 * t + b][:, :].rearrange("p (k n) -> p k n", k=4), uT_hi[sl]).then_inc(ul, 1)

            def input_lo(t, b):
                dve.wait_ge(uh, NT * b + t + 1)
                sl = (slice(None), slice(4 * b, 4 * b + 4), slice(P * t, P * t + P))
                lo_part(uT_lo[sl], ps[4 + t][:, :].rearrange("p (k n) -> p k n", k=4), uT_hi[sl]).then_inc(ul, 1)

            input_lo(0, 0)
            in_lo(0)
            input_lo(1, 0)
            input_lo(2, 0)
            input_lo(3, 0)
            in_lo(1)
            input_lo(0, 1)
            input_lo(1, 1)
            input_lo(2, 1)
            input_lo(3, 1)
            in_lo(2)
            in_lo(3)
            dve.wait_ge(lat_in, 32)
            for t in range(NT):
                dve.wait_ge(kr_c, t + 1)
                for norm, c0, n in ((1, 0, QR), (2, QR, KVR)):
                    dve.wait_ge(rstd, NT + 2 * t + norm)
                    nc.vector.scalar_tensor_tensor(out=cn[:, t, c0:c0 + n], in0=ps[t][:, c0:c0 + n],
                                                   scalar=stat[:, norm, t, 3:4], in1=lat_g[:, c0:c0 + n],
                                                   op0=ALU.mult, op1=ALU.mult).then_inc(cn_ready, 1)
            dve.wait_ge(tab_in, 16)
            cosM, sinM = rope_sb[:, :, 0:32], rope_sb[:, :, 32:96]
            cosL, sinL = rope_sb[:, :, 96:112], rope_sb[:, :, 112:144]

            def pairs(a, d):
                return a.rearrange("p t (s d) -> p t s d", s=2, d=d)

            k4 = pairs(kr[:, :, :], 16)
            m1 = rt1[:, 0, 0:NT * ROPE].rearrange("p (t s d) -> p t s d", t=NT, s=2)
            m2 = rt2[:, 0, 0:NT * ROPE].rearrange("p (t s d) -> p t s d", t=NT, s=2)
            nc.vector.tensor_tensor(m1, k4, cosL.unsqueeze(2).to_broadcast([P, NT, 2, 16]), ALU.mult)
            nc.vector.tensor_tensor(m2[:, :, 0, :], k4[:, :, 1, :], sinL[:, :, 0:16], ALU.mult)
            step(nc.vector.tensor_tensor(m2[:, :, 1, :], k4[:, :, 0, :], sinL[:, :, 16:32], ALU.mult))
            nc.vector.tensor_tensor(pairs(krr[:, :, :], 16), m1, m2, ALU.add).then_inc(krr_ready, 1)
            dve.wait_ge(krr_ready, 1)

            def rotate(n):
                t, group = n % NT, 1 + n // NT
                r = stat[:, 0, t, 3:4]
                dve.wait_ge(proj, NT * group + t + 1)
                if n >= 2:
                    dve.wait_ge(roped, n - 1)
                src = ps[4 + t][:, :].rearrange("p (h s d) -> p h s d", h=HEADS, s=2)
                o1 = rt1[:, n % 2, :].rearrange("p (g d) -> p g d", d=32)
                o2 = rt2[:, n % 2, :].rearrange("p (h s d) -> p h s d", h=HEADS, s=2)

                def product(o, i, table, g):
                    return nc.vector.scalar_tensor_tensor(out=o, in0=i, scalar=r, op0=ALU.mult, op1=ALU.mult,
                                                          in1=table.unsqueeze(1).to_broadcast([P, g, 32]))

                product(o1, ps[4 + t][:, :].rearrange("p (g d) -> p g d", d=32), cosM[:, t, :], 2 * HEADS)
                for s in range(2):
                    last = product(o2[:, :, s, :], src[:, :, 1 - s, :], sinM[:, t, 32 * s:32 * s + 32], HEADS)
                last.then_inc(rope_m, 1)

            in_lo(4)
            for t in range(NT):
                rotate(t)
            for j in range(3):
                dve.wait_ge(ch, j + 1)
                lo_part(cT_lo[:, j, :], ps[j][:, :], cT_hi[:, j, :]).then_inc(cl, 1)
            dve.wait_ge(krh, 2)
            for i in range(2):
                lo_part(kT_lo[i][NOPE:QH, :], ps[3][0:ROPE, :], kT_hi[i][NOPE:QH, :]).then_inc(krl, 1)
            in_lo(5)
            dve.wait_ge(wh_ready, Q_CH + 1)
            w = slice(0, 2 * HEADS * QH)
            lo_part(w_lo[Q_CH % 2][:, w], raw[Q_CH % 2][:, w], w_hi[Q_CH % 2][:, w]).then_inc(w_ready, 1)
            dve.wait_ge(wh_ready, KV_CH + 1)
            lo_part(wkv_lo[:, :], raw[KV_CH % 2][:, 0:HEADS * P], wkv_hi[:, :]).then_inc(w_ready, 1)
            for t in range(NT):
                rotate(NT + t)
            in_lo(6)
            dve.wait_ge(roped, 2 * NT)
            for t in range(NT):
                dve.wait_ge(qup_c, 2 * t + 2)
                q4 = q_nat[:, t, :].rearrange("p (h c) -> p h c", c=QH)[:, :, NOPE:QH].rearrange("p h (s d) -> p h s d", s=2)
                m1 = rt1[:, t % 2, 0:HEADS * ROPE].rearrange("p (h s d) -> p h s d", h=HEADS, s=2)
                m2 = rt2[:, t % 2, 0:HEADS * ROPE].rearrange("p (h s d) -> p h s d", h=HEADS, s=2)
                cs = cosL[:, t, :].unsqueeze(1).unsqueeze(1).to_broadcast([P, HEADS, 2, 16])
                nc.vector.tensor_tensor(m1, q4, cs, ALU.mult)
                for s in range(2):
                    last = nc.vector.tensor_tensor(m2[:, :, s, :], q4[:, :, 1 - s, :],
                                                   sinL[:, t, 16 * s:16 * s + 16].unsqueeze(1).to_broadcast([P, HEADS, 16]),
                                                   ALU.mult)
                step(last)
                nc.vector.tensor_tensor(q4, m1, m2, ALU.add).then_inc(q_roped, 1)
            for t in range(NT):
                dve.wait_ge(vh, t + 1)
                lo_part(v_lo[:, 0, t, :], ps[t][:, :], v_hi[:, 0, t, :]).then_inc(vl, 1)
            in_lo(7)

            def maxes(i, tiles):
                for t in tiles:
                    n = S_ORDER.index(t)
                    b, c = S_AT[t]
                    dve.wait_ge(s_full, 3 * i + min(n + 1, 3))
                    last = nc.vector.reduce_max(mx[:, i % 2, t:t + 1], ps[b][:, c:c + P * (t + 1)], AX_X)
                    if n in (0, 3):
                        step(last)
                        w = slice(t, t + 1) if n == 0 else slice(0, 3)
                        nc.vector.tensor_scalar(nb[:, i % 2, w], mx[:, i % 2, w], -SCALE[i], None,
                                                ALU.mult).then_inc(s_nb, 1)

            def inverse_sums(i):
                for n, w in enumerate((slice(3, 4), slice(0, 3))):
                    dve.wait_ge(s_exp, NT * i + (1, NT)[n])
                    if i >= 2:
                        dve.wait_ge(s_norm, NT * (i - 1))
                    nc.vector.reciprocal(ri[:, i % 2, w], rs[:, i % 2, w]).then_inc(s_ri, 1)

            def q_part(i):
                if prepared(i):
                    dve.wait_ge(qh, preps(i))
                    rows = QH if i < HEADS else P
                    s = slot(i)
                    lo_part(qT_lo[s][0:rows, :], ps[qk_banks(i)[0]][0:rows, :], qT_hi[s][0:rows, :]).then_inc(ql, 1)

            def k_part(i):
                if prepared(i):
                    dve.wait_ge(kh, preps(i))
                    rows = NOPE if i < HEADS else P
                    s = slot(i)
                    lo_part(kT_lo[s][0:rows, :], ps[qk_banks(i)[1]][0:rows, :], kT_hi[s][0:rows, :]).then_inc(kl, 1)

            def p_part(i):
                for n, (b, c, w) in enumerate(PT_COPY):
                    dve.wait_ge(ph, 3 * i + n + 1)
                    lo_part(pT_lo[i % 2][:, c:c + w], ps[b][:, 0:w], pT_hi[i % 2][:, c:c + w]).then_inc(pl, 1)

            def o_part(i):
                dve.wait_ge(oh, i + 1)
                r0 = VD * (i % 2)
                lo_part(uT_lo[r0:r0 + VD, i // 2, :], ps[6][0:VD, :], uT_hi[r0:r0 + VD, i // 2, :]).then_inc(ol, 1)

            for i in (0, 1):
                q_part(i)
                k_part(i)
            maxes(0, S_ORDER)
            inverse_sums(0)
            for t in range(NT):
                if t == 3:
                    maxes(1, S_ORDER[:1])
                    q_part(2)
                    maxes(1, S_ORDER[1:])
                    k_part(2)
                dve.wait_ge(vh, NT + t + 1)
                lo_scaled(v_lo[:, 1, t, :], ps[4 + t][:, :], stat[:, 0, t, 3:4], v_hi[:, 1, t, :]).then_inc(vl, 1)
            inverse_sums(1)
            p_part(0)
            for i in range(1, NH + 2):
                if 2 <= i < NH:
                    inverse_sums(i)
                if HEADS <= i < NH - 1:
                    maxes(i + 1, S_ORDER[:1])
                if 2 <= i <= NH:
                    p_part(i - 1)
                if i < HEADS:
                    maxes(i + 1, S_ORDER)
                k_part(i + 2)
                q_part(i + 2)
                if HEADS <= i < NH - 1:
                    maxes(i + 1, S_ORDER[1:])
                if i >= 2:
                    o_part(i - 2)

            def mlp_lo(j, r, gains=True):
                dve.wait_ge(wh_ready, r + (1 - NO))
                if gains:
                    for k in range(ND):
                        w = slice(256 * k, 256 * k + 256)
                        last = lo_scaled(w_lo[1 - j][:, w], raw[j][:, w], g_up[:, k:k + 1], w_hi[1 - j][:, w])
                else:
                    last = lo_part(w_lo[1 - j][:, :], raw[j][:, :], w_hi[1 - j][:, :])
                last.then_inc(w_ready, 1)

            for j in range(2):
                mlp_lo(j, UP_CH + j)

            halves = [0]

            def scaled(norm, t, n_sq, n_rstd, n_g, by=None):
                dve.wait_ge(g_post_in, n_g)
                for b in range(2):
                    w = slice(TOP * b, TOP * b + TOP)
                    if halves[0] >= 2:
                        dve.wait_ge(h_ready, halves[0] - 1)
                    halves[0] += 1
                    dve.wait_ge(sq, n_sq + b)
                    if by is None:
                        last = nc.vector.tensor_tensor(un[:, w], ps[2 * t + b][:, :], post_g[:, w], ALU.mult)
                    else:
                        last = nc.vector.scalar_tensor_tensor(out=un[:, w], in0=ps[2 * t + b][:, :], scalar=by,
                                                              in1=post_g[:, w], op0=ALU.mult, op1=ALU.mult)
                    last.then_inc(y_s, 1)
                dve.wait_ge(rstd, n_rstd)
                for b in range(2):
                    w = slice(TOP * b, TOP * b + TOP)
                    dve.wait_ge(y_s, halves[0] - 1 + b)
                    nc.vector.scalar_tensor_tensor(out=h_sb[:, t, w], in0=un[:, w], scalar=stat[:, norm, t, 3:4],
                                                   in1=h_sb[:, t, w], op0=ALU.mult, op1=ALU.add).then_inc(h_ready, 1)

            for t in range(NT):
                dve.wait_ge(h_in[t], 16)
                scaled(3, t, 3 * NT + 2 * t + 1, 3 * NT + t + 1, 16)
                if t >= 1:
                    transposed_lo(2 * NT, t - 1)
            transposed_lo(2 * NT, NT - 1)

            def up_step(i, first=False, last=False):
                for j in range(2):
                    if not (first and j == 0):
                        mlp_lo(1 - j, i * 2 + (UP_CH + j + 1), not (last and j == 1))
                    for m in range(2):
                        dve.wait_ge(relu_c, i * 4 + (2 * j + m + 1))
                        nc.vector.tensor_tensor(act_sb[:, bass.ds(i * 4 + (2 * j + m), 1), :], relu[:, m:m + 1, :],
                                                relu[:, m:m + 1, :], ALU.mult).then_inc(a_ready, 1)

            def down_a(j, c):
                dve.wait_ge(ah, c + 1)
                lo_part(a_lo[j][:, :, :], act_sb[:, bass.ds(c * 2, 2), :], a_hi[j][:, :, :]).then_inc(al, 1)

            up_step(0, first=True)
            down_a(0, 0)
            with dve.Fori(1, NF // 4 - 1) as i:
                up_step(i)
            up_step(NF // 4 - 1, last=True)

            def down_lo(j, c):
                mlp_lo(j, c + DOWN_CH, False)
                down_a(j, c)

            down_lo(1, 1)
            with dve.Fori(1, NF // 4) as i:
                for j in range(2):
                    down_lo(j, i * 2 + j)
            for t in range(NT):
                scaled(5, t, 6 * NT + 2 * t + 1, 5 * NT + t + 1, 32, stat[:, 4, t, 3:4])

        @block.tensor
        def _(pe):
            def mm3(out, lh, ll, rh, rl, start, stop):
                nc.tensor.matmul(out, lh, rh, start=start, stop=False)
                nc.tensor.matmul(out, lh, rl, start=False, stop=False)
                return nc.tensor.matmul(out, ll, rh, start=False, stop=stop)

            def transposes(src, t):
                for k in range(ND):
                    last = nc.tensor.transpose(ps[2 * t + k // 4][:, P * (k % 4):P * (k % 4) + P],
                                               src[:, t, P * k:P * k + P], ident[:, :])
                    if k % 4 == 3:
                        last.then_inc(uT_full, 1)

            def group(g, before_tile):
                n = GROUP_COLS[g][1]
                for part in range(2):
                    r = IN_CH[2 * g + part]
                    for t in range(NT):
                        before_tile(part, t)
                        if t == 0:
                            pe.wait_ge(*((first_ready, 1) if r == 0 else (w_ready, r + 1)))
                        tok = slice(P * t, P * t + P)
                        for k in range(4):
                            if r == 0 and t == 0 and k >= 1:
                                pe.wait_ge(*((first_ready, k + 1) if k < 3 else (w_ready, 1)))
                            w = slice(n * k, n * k + n)
                            last = mm3(ps[4 * (g > 0) + t][:, 0:n], uT_hi[:, 4 * part + k, tok], uT_lo[:, 4 * part + k, tok],
                                       w_hi[w_slot(r)][:, w], w_lo[w_slot(r)][:, w], part == 0 and k == 0, part == 1 and k == 3)
                        if part == 1:
                            last.then_inc(proj, 1)
                    if part == 0:
                        last.then_inc(w_used, 1)

            def input_half(t, b):
                pe.wait_ge(x_in[t][b], 16)
                if b == 1:
                    pe.wait_ge(ul, t + 1)
                for k in range(4):
                    c = TOP * b + P * k
                    last = nc.tensor.transpose(ps[4 + t][:, P * k:P * k + P], x_sb[:, t, c:c + P], ident[:, :])
                last.then_inc(uT_full, 1)

            def warm(n):
                for _ in range(n):
                    nc.tensor.matmul(ps[0][:, 0:P], ident_b[:, :], ident_b[:, :], start=True, stop=True)

            def before_latents(part, t):
                n = NT * part + t
                for m in {0: (0, 1), 1: (2, 3)}.get(n, (n + 2,)):
                    if m < 2 * NT:
                        input_half(m % NT, m // NT)
                    if m == 0:
                        warm(24)
                pe.wait_ge(ul, n + 1)

            pe.wait_ge(consts, 3)
            warm(12)
            group(0, before_latents)
            group(1, lambda part, t: None)
            pe.wait_ge(cn_ready, 2 * NT)
            for j in range(3):
                for t in range(NT):
                    last = nc.tensor.transpose(ps[j][:, P * t:P * t + P], cn[:, t, P * j:P * j + P], ident[:, :])
                last.then_inc(cT_full, 1)
            pe.wait_ge(krr_ready, 1)
            for t in range(NT):
                last = nc.tensor.transpose(ps[3][0:ROPE, P * t:P * t + P], krr[:, t, :], ident[:, :])
            last.then_inc(krT_full, 1)
            group(2, lambda part, t: part == 0 and pe.wait_ge(rope_m, t + 1))
            pe.wait_ge(w_ready, Q_CH + 1)
            pe.wait_ge(cl, 3)
            pe.wait_ge(krl, 2)
            for n in range(2 * NT):
                t, hf = n // 2, n % 2
                if n >= NT:
                    pe.wait_ge(rope_m, n + 1)
                for k in range(2):
                    w = slice(HEADS * QH * k + 4 * QH * hf, HEADS * QH * k + 4 * QH * (hf + 1))
                    last = mm3(ps[n][:, 0:4 * QH], cT_hi[:, k, P * t:P * t + P], cT_lo[:, k, P * t:P * t + P],
                               w_hi[Q_CH % 2][:, w], w_lo[Q_CH % 2][:, w], k == 0, k == 1)
                last.then_inc(qup, 1)
            pe.wait_ge(w_ready, KV_CH + 1)
            wv_hi = wkv_hi[:, :].rearrange("p (h c) -> p h c", c=P)[:, :, NOPE:]
            wv_lo = wkv_lo[:, :].rearrange("p (h c) -> p h c", c=P)[:, :, NOPE:]
            for t in range(NT):
                pe.wait_ge(qup_c, t + 1)
                last = mm3(ps[t][:, :].rearrange("p (h c) -> p h c", c=VD), cT_hi[:, 2, P * t:P * t + P],
                           cT_lo[:, 2, P * t:P * t + P], wv_hi, wv_lo, True, True)
                last.then_inc(v_full, 1)

            def q_prep(i):
                if prepared(i):
                    if i == 0:
                        pe.wait_ge(vl, NT)
                        pe.wait_ge(q_roped, NT)
                    elif i >= 3:
                        pe.wait_ge(pl, 3 * (i - 3) + 1)
                    if i == HEADS:
                        pe.wait_ge(roped, 2 * NT)
                    b, rows = qk_banks(i)[0], QH if i < HEADS else P
                    src, c0 = (q_nat, QH * i) if i < HEADS else (mq_nat, MOBA_D * (i - HEADS))
                    for t in range(NT):
                        last = nc.tensor.transpose(ps[b][0:rows, P * t:P * t + P], src[:, t, c0:c0 + rows], ident[:, :])
                    last.then_inc(qT_full, 1)

            def k_prep(i):
                if prepared(i):
                    b = qk_banks(i)[1]
                    if i in (2, 3):
                        pe.wait_ge(vl, NT + i + 1)
                    elif i > 3:
                        pe.wait_ge(kl, preps(i) - 1)
                    if i < HEADS:
                        w = slice(P * i, P * i + P)
                        last = mm3(ps[b][:, :], wkv_hi[:, w], wkv_lo[:, w], cT_hi[:, 2, :], cT_lo[:, 2, :], True, True)
                    else:
                        c0 = MOBA_D * (i - HEADS)
                        for t in range(NT):
                            last = nc.tensor.transpose(ps[b][:, P * t:P * t + P], mk_nat[:, t, c0:c0 + P], ident[:, :])
                    last.then_inc(kT_full, 1)

            def scores(i):
                pe.wait_ge(kl, 2 if i == 0 else preps(i))
                s, r = slot(i), slice(0, QH)
                if i >= HEADS:
                    r = slice(MOBA_D * (i % 2), MOBA_D * (i % 2) + MOBA_D)
                for n, t in enumerate(S_ORDER):
                    b, c = S_AT[t]
                    if i >= 1:
                        pe.wait_ge(s_exp, NT * (i - 1) + (n + 1 if n < 2 else NT))
                    w, tok = P * (t + 1), slice(P * t, P * t + P)
                    mm3(ps[b][:, c:c + w], qT_hi[s][r, tok], qT_lo[s][r, tok], kT_hi[s][r, 0:w], kT_lo[s][r, 0:w],
                        True, False)
                    last = nc.tensor.matmul(ps[b][:, c + w - P:c + w], ident_b[:, :], mask_b[:, :], start=False, stop=True)
                    if n != 2:
                        last.then_inc(s_full, 1)

            def before_values(part, t):
                if part == 0:
                    pe.wait_ge(qup_c, NT + t + 1)
                elif t == 0:
                    for i in (0, 1):
                        q_prep(i)
                        k_prep(i)
                elif t == 2:
                    scores(0)
                elif t == 3:
                    q_prep(2)
                    scores(1)
                    k_prep(2)

            group(3, before_values)

            def probs_T(i):
                pe.wait_ge(s_norm, NT * (i + 1))
                for k in PT_ORDER:
                    b, c = PT_AT[k]
                    if k == 0:
                        j = max(j for j in range(min(i + 3, NH)) if prepared(j))
                        pe.wait_ge(ql, preps(j))
                    if i == 0 and k == 0:
                        pe.wait_ge(vl, NT + 2)
                    if i >= 1 and k < 3:
                        pe.wait_ge(pl, 3 * (i - 1) + k + 1)
                    for t in range(k, NT):
                        last = nc.tensor.transpose(ps[b][:, c + P * (t - k):c + P * (t - k) + P],
                                                   probs[i % 2][:, p_off(t) + P * k:p_off(t) + P * k + P], ident[:, :])
                    if k != 1:
                        last.then_inc(pT_full, 1)

            def weighted(i):
                pe.wait_ge(pl, 3 * (i + 1))
                if i >= 1:
                    pe.wait_ge(ol, i)
                g, vc = i // HEADS, slice(VD * (i % HEADS), VD * (i % HEADS) + VD)
                for k in range(NT):
                    w = slice(PT_OFF[k], PT_OFF[k] + P * (NT - k))
                    out_k, stop = ps[6][:, P * k:TOP], k == NT - 1
                    last = mm3(out_k[0:VD], v_hi[:, g, k, vc], v_lo[:, g, k, vc], pT_hi[i % 2][:, w], pT_lo[i % 2][:, w], k == 0, stop)
                last.then_inc(o_full, 1)

            def out_rows(t, b, c, kk):
                tok, k = slice(P * t, P * t + P), 2 * c + kk
                s = w_slot(OUT_CH[c])
                hi, lo = (w_hi[s], w_lo[s]) if c < 2 else (wo_hi[c - 2], wo_lo[c - 2])
                w = slice(D * kk + TOP * b, D * kk + TOP * b + TOP)
                return mm3(ps[2 * t + b][:, :], uT_hi[:, k, tok], uT_lo[:, k, tok], hi[:, w], lo[:, w], k == 0, k == ND - 1)

            def out_tile(t, c):
                for kk in range(2):
                    for b in range(2):
                        last = out_rows(t, b, c, kk)
                return last

            def out_early(c):
                pe.wait_ge(wo_ready, c + 1)
                pe.wait_ge(s_exp, NT * NH)
                pe.wait_ge(ol, 4 * (c + 1))
                out_tile(0, c)

            probs_T(0)
            for i in range(1, NH + 2):
                if i == NH:
                    out_early(0)
                if 2 <= i <= NH:
                    probs_T(i - 1)
                if i == 2:
                    k_prep(4)
                if i + 1 < NH:
                    scores(i + 1)
                q_prep(i + 2)
                if i == NH + 1:
                    out_early(1)
                if i >= 3:
                    weighted(i - 2)
                k_prep(3 if i == 1 else i + 3)
                if i == 1:
                    weighted(0)

            for c in range(2):
                for t in range(1, NT):
                    if c == 0 and t == NT - 1:
                        pe.wait_ge(ol, NH)
                    last = out_tile(t, c)
                last.then_inc(w_used, 1)
            pe.wait_ge(wo_ready, NO)
            for t in range(NT):
                for b in range(2):
                    for c in (2, 3):
                        for kk in range(2):
                            last = out_rows(t, b, c, kk)
                    last.then_inc(y_full, 1)
                if t >= 1:
                    pe.wait_ge(h_ready, 2 * t)
                    transposes(h_sb, t - 1)

            def up_block(bank, j, m, tok):
                for k in range(ND):
                    w = slice(256 * k + P * m, 256 * k + P * m + P)
                    last = mm3(ps[bank][:, tok], w_hi[1 - j][:, w], w_lo[1 - j][:, w], uT_hi[:, k, tok], uT_lo[:, k, tok],
                               k == 0, k == ND - 1)
                return last

            A, B = slice(0, 2 * P), slice(2 * P, 4 * P)
            pe.wait_ge(w_ready, UP_CH + 2 - NO)
            pe.wait_ge(ul, 2 * NT + 4)
            up_block(0, 0, 0, A)
            up_block(1, 0, 1, A)
            pe.wait_ge(h_ready, 2 * NT)
            transposes(h_sb, NT - 1)
            up_block(2, 1, 0, A)
            pe.wait_ge(ul, 4 * NT)
            for bank in range(3):
                up_block(bank, bank // 2, bank % 2, B).then_inc(up_full, 1)
            up_block(3, 1, 1, slice(0, S)).then_inc(up_full, 1)
            with pe.Fori(1, NF // 4) as i:
                for j in range(2):
                    pe.wait_ge(w_ready, i * 2 + (UP_CH + j + 1 - NO))
                    for m in range(2):
                        pe.wait_ge(relu_c, i * 4 + (2 * j + m - 3))
                        up_block(2 * j + m, j, m, slice(0, S)).then_inc(up_full, 1)

            def down_rows(t, b, j, kk, start, stop):
                tok = slice(P * t, P * t + P)
                w = slice(D * kk + TOP * b, D * kk + TOP * b + TOP)
                return mm3(ps[2 * t + b][:, :], a_hi[j][:, kk, tok], a_lo[j][:, kk, tok], w_hi[1 - j][:, w], w_lo[1 - j][:, w],
                           start, stop)

            def down_chunk(j, c, first=False):
                pe.wait_ge(w_ready, c + (DOWN_CH + 1 - NO))
                pe.wait_ge(al, c + 1)
                for t in ((2, 3, 0, 1) if first else range(NT)):
                    if first and t < 2:
                        pe.wait_ge(relu_c, NF - 2 * (1 - t))
                    for kk in range(2):
                        for b in range(2):
                            last = down_rows(t, b, j, kk, first and kk == 0, False)
                last.then_inc(w_used, 1)

            down_chunk(0, 0, True)
            down_chunk(1, 1)
            with pe.Fori(1, NF // 4 - 1) as i:
                down_chunk(0, i * 2)
                down_chunk(1, i * 2 + 1)
            def last_rows(t, j, b):
                for kk in range(2):
                    last = down_rows(t, b, j, kk, False, j == 1 and kk == 1)
                return last

            pe.wait_ge(w_ready, DOWN_CH - NO + NF // 2 - 1)
            pe.wait_ge(al, NF // 2 - 1)
            for t in (0, 1):
                for b in range(2):
                    last_rows(t, 0, b)
            pe.wait_ge(w_ready, DOWN_CH - NO + NF // 2)
            pe.wait_ge(al, NF // 2)
            for t in range(NT):
                for b in range(2):
                    if t >= 2:
                        last_rows(t, 0, b)
                    last_rows(t, 1, b).then_inc(y_full, 1)


def rope_constants(seq):
    import numpy as np

    cols = []
    for half in (MOBA_D // 2, ROPE // 2):
        inv = (np.float32(1.0) / np.float32(10000.0) ** (np.arange(half, dtype=np.float32) / np.float32(half))).astype(np.float32)
        ang = (np.arange(seq, dtype=np.float32)[:, None] * inv[None, :]).astype(np.float32)
        c, s = np.cos(ang).astype(np.float32), np.sin(ang).astype(np.float32)
        cols += [c, -s, s]
    return np.ascontiguousarray(np.concatenate(cols, axis=1))


NAMES = ["x", "attn_pre_g", "w_in", "mla_q_norm_g", "w_mla_q_up", "mla_kv_norm_g", "w_mla_kv_up", "w_out",
         "attn_post_g", "mlp_pre_g", "w_up", "w_down", "mlp_post_g"]


def kernel(**inputs):
    import numpy as np
    import concourse.bacc as bacc
    from concourse.bass_utils import run_bass_kernel_spmd

    nc = bacc.Bacc("TRN2", target_bir_lowering=False, num_devices=1)
    arrays = {name: np.ascontiguousarray(inputs[name]) for name in NAMES}
    arrays["rope_table"] = rope_constants(arrays["x"].shape[1])
    args = [nc.dram_tensor(f"in_{name}", a.shape, mybir.dt.from_np(a.dtype), kind="ExternalInput").ap()
            for name, a in arrays.items()]
    out = nc.dram_tensor("out", arrays["x"].shape, F32, kind="ExternalOutput").ap()
    build(nc, *args, out)
    r = run_bass_kernel_spmd(nc, [{f"in_{name}": a for name, a in arrays.items()}], core_ids=[0])
    return r.results[0]["out"]
```
